# Optimizing a Trainium2 kernel written in Bass

```python
import jax, jax.numpy as jnp
from jax import lax
import numpy as np

D_MODEL = 1024
BATCH = 1
SEQ = 512
DEPTH = 1

LRU_WIDTH = 512
LRU_BLOCKS = 8
LRU_BLOCK_DIM = LRU_WIDTH // LRU_BLOCKS
LRU_CONV = 4
LRU_C = 8.0
N_HEADS = 8
HEAD_DIM = 64
ATT_WIDTH = N_HEADS * HEAD_DIM
MIX_WIDTH = LRU_WIDTH + ATT_WIDTH
IN_WIDTH = 2 * LRU_WIDTH + 3 * ATT_WIDTH
MOBA_BLOCK = 256
MOBA_TOPK = 3
Q_CHUNK = 32
D_FF = 3072
FFN_CONV = 3
PLE_DIM = 256
EPS = 1e-6
NEG = -1e30

kernel_name = "hymba_rglru_moba_convffn_ple"

def rmsnorm(x, g):
    xf = x.astype(jnp.float32)
    y = xf * lax.rsqrt(jnp.mean(xf * xf, axis=-1, keepdims=True) + EPS)
    return (y * g.astype(jnp.float32)).astype(x.dtype)

def causal_dwconv(x, w, b):
    K, C = w.shape
    y = lax.conv_general_dilated(
        x, w.reshape(K, 1, C).astype(x.dtype), window_strides=(1,), padding=[(K - 1, 0)],
        dimension_numbers=("NWC", "WIO", "NWC"), feature_group_count=C)
    return y + b.astype(x.dtype)

def rglru(xc, wa, ba, wx, bx, lam):
    B, T, W = xc.shape
    xb = xc.reshape(B, T, LRU_BLOCKS, LRU_BLOCK_DIM)
    r = jax.nn.sigmoid(jnp.einsum("btnc,ncd->btnd", xb, wa).reshape(B, T, W) + ba)
    i = jax.nn.sigmoid(jnp.einsum("btnc,ncd->btnd", xb, wx).reshape(B, T, W) + bx)
    log_a = -LRU_C * r.astype(jnp.float32) * jax.nn.softplus(-lam.astype(jnp.float32))
    a = jnp.exp(log_a)
    mult = jnp.sqrt(-jnp.expm1(2.0 * log_a))
    mult = mult.at[:, 0].set(1.0)
    b = mult * (i * xc).astype(jnp.float32)

    def combine(left, right):
        a1, b1 = left
        a2, b2 = right
        return a1 * a2, a2 * b1 + b2

    _, hs = lax.associative_scan(combine, (a, b), axis=1)
    return hs.astype(xc.dtype)

def moba_attention(q, k, v, slopes):
    B, T, H, Dh = q.shape
    L = MOBA_BLOCK
    NB = -(-T // L)
    Tp = NB * L
    if Tp != T:
        pad = ((0, 0), (0, Tp - T), (0, 0), (0, 0))
        q, k, v = jnp.pad(q, pad), jnp.pad(k, pad), jnp.pad(v, pad)
    scale = 1.0 / np.sqrt(Dh)
    qh = q.transpose(0, 2, 1, 3)
    kb = k.transpose(0, 2, 1, 3).reshape(B, H, NB, L, Dh)
    vb = v.transpose(0, 2, 1, 3).reshape(B, H, NB, L, Dh)

    k_mean = jnp.mean(kb.astype(jnp.float32), axis=3)
    gate = jnp.einsum("bhtd,bhnd->bhtn", qh.astype(jnp.float32), k_mean)
    q_blk = jnp.arange(Tp) // L
    past = jnp.arange(NB)[None, :] < q_blk[:, None]
    gate = jnp.where(past[None, None], gate, NEG)
    n_sel = min(MOBA_TOPK, NB)
    _, sel = lax.top_k(gate, n_sel)
    valid = jnp.arange(n_sel)[None, :] < jnp.minimum(q_blk, n_sel)[:, None]

    n_chunks = Tp // Q_CHUNK
    q_c = qh.reshape(B, H, n_chunks, Q_CHUNK, Dh).transpose(2, 0, 1, 3, 4)
    sel_c = sel.reshape(B, H, n_chunks, Q_CHUNK, n_sel).transpose(2, 0, 1, 3, 4)
    valid_c = valid.reshape(n_chunks, Q_CHUNK, n_sel)
    idx_c = jnp.arange(n_chunks, dtype=jnp.int32)
    bi = jnp.arange(B)[:, None, None, None]
    hi = jnp.arange(H)[None, :, None, None]
    slope_f = slopes.astype(jnp.float32)

    def body(args):
        qc, selc, validc, c = args
        t_pos = c * Q_CHUNK + jnp.arange(Q_CHUNK)
        qb = (c * Q_CHUNK) // L
        ks = kb[bi, hi, selc]
        vs = vb[bi, hi, selc]
        s_pos = selc[..., None] * L + jnp.arange(L)
        dist_sel = (t_pos[None, None, :, None, None] - s_pos).astype(jnp.float32)
        lg_sel = jnp.einsum("bhcd,bhcsld->bhcsl", qc, ks, preferred_element_type=jnp.float32) * scale
        lg_sel = lg_sel - slope_f[None, :, None, None, None] * dist_sel
        lg_sel = jnp.where(validc[None, None, :, :, None], lg_sel, NEG)
        k_own = lax.dynamic_index_in_dim(kb, qb, axis=2, keepdims=False)
        v_own = lax.dynamic_index_in_dim(vb, qb, axis=2, keepdims=False)
        s_own = qb * L + jnp.arange(L)
        dist_own = (t_pos[:, None] - s_own[None, :]).astype(jnp.float32)
        lg_own = jnp.einsum("bhcd,bhld->bhcl", qc, k_own, preferred_element_type=jnp.float32) * scale
        lg_own = lg_own - slope_f[None, :, None, None] * dist_own[None, None]
        lg_own = jnp.where((dist_own >= 0)[None, None], lg_own, NEG)
        logits = jnp.concatenate([lg_sel.reshape(B, H, Q_CHUNK, n_sel * L), lg_own], axis=-1)
        w = jax.nn.softmax(logits, axis=-1).astype(vb.dtype)
        w_sel = w[..., : n_sel * L].reshape(B, H, Q_CHUNK, n_sel, L)
        w_own = w[..., n_sel * L:]
        out = (jnp.einsum("bhcsl,bhcsld->bhcd", w_sel, vs, preferred_element_type=jnp.float32)
               + jnp.einsum("bhcl,bhld->bhcd", w_own, v_own, preferred_element_type=jnp.float32))
        return out.astype(vb.dtype)

    out = lax.map(body, (q_c, sel_c, valid_c, idx_c))
    out = out.transpose(1, 0, 3, 2, 4).reshape(B, Tp, H * Dh)
    return out[:, :T]

def setup_inputs(seed: int = 0) -> dict:
    key = jax.random.key(seed)
    ks = jax.random.split(key, 24)
    f32 = jnp.float32

    def nrm(k, shape, scale):
        return jax.random.normal(k, shape, f32) * scale

    def gain(k, shape):
        return 1.0 + 0.05 * jax.random.normal(k, shape, f32)

    u = jax.random.uniform(ks[9], (DEPTH, LRU_WIDTH), f32, 0.9, 0.999)
    a0 = u ** (1.0 / LRU_C)
    lru_lambda = jnp.log(a0) - jnp.log1p(-a0)
    return {
        "x": nrm(ks[0], (BATCH, SEQ, D_MODEL), 1.0),
        "p": nrm(ks[1], (DEPTH, BATCH, SEQ, PLE_DIM), 1.0),
        "ln_mix": gain(ks[2], (DEPTH, D_MODEL)),
        "w_in": nrm(ks[3], (DEPTH, D_MODEL, IN_WIDTH), D_MODEL ** -0.5),
        "conv_w": nrm(ks[4], (DEPTH, LRU_CONV, LRU_WIDTH), LRU_CONV ** -0.5),
        "conv_b": nrm(ks[5], (DEPTH, LRU_WIDTH), 0.01),
        "gate_a_w": nrm(ks[6], (DEPTH, LRU_BLOCKS, LRU_BLOCK_DIM, LRU_BLOCK_DIM), LRU_BLOCK_DIM ** -0.5),
        "gate_a_b": nrm(ks[7], (DEPTH, LRU_WIDTH), 0.01),
        "gate_x_w": nrm(ks[8], (DEPTH, LRU_BLOCKS, LRU_BLOCK_DIM, LRU_BLOCK_DIM), LRU_BLOCK_DIM ** -0.5),
        "gate_x_b": nrm(ks[10], (DEPTH, LRU_WIDTH), 0.01),
        "lru_lambda": lru_lambda,
        "q_gain": gain(ks[11], (DEPTH, HEAD_DIM)),
        "k_gain": gain(ks[12], (DEPTH, HEAD_DIM)),
        "w_out": nrm(ks[13], (DEPTH, MIX_WIDTH, D_MODEL), MIX_WIDTH ** -0.5),
        "ln_ffn": gain(ks[14], (DEPTH, D_MODEL)),
        "w_up": nrm(ks[15], (DEPTH, D_MODEL, 2 * D_FF), D_MODEL ** -0.5),
        "ffn_conv_w": nrm(ks[16], (DEPTH, FFN_CONV, D_FF), FFN_CONV ** -0.5),
        "ffn_conv_b": nrm(ks[17], (DEPTH, D_FF), 0.01),
        "w_down": nrm(ks[18], (DEPTH, D_FF, D_MODEL), D_FF ** -0.5),
        "ln_ple": gain(ks[19], (DEPTH, D_MODEL)),
        "w_ple_gate": nrm(ks[20], (DEPTH, D_MODEL, D_MODEL), D_MODEL ** -0.5),
        "w_ple_proj": nrm(ks[21], (DEPTH, PLE_DIM, D_MODEL), PLE_DIM ** -0.5),
    }

def reference(x, p, ln_mix, w_in, conv_w, conv_b, gate_a_w, gate_a_b, gate_x_w, gate_x_b,
              lru_lambda, q_gain, k_gain, w_out, ln_ffn, w_up, ffn_conv_w, ffn_conv_b, w_down,
              ln_ple, w_ple_gate, w_ple_proj):
    B, T, _ = x.shape
    slopes = 2.0 ** (-8.0 * jnp.arange(1, N_HEADS + 1, dtype=jnp.float32) / N_HEADS)
    split_at = [LRU_WIDTH, 2 * LRU_WIDTH, 2 * LRU_WIDTH + ATT_WIDTH, 2 * LRU_WIDTH + 2 * ATT_WIDTH]
    h = x
    for i in range(DEPTH):
        u = rmsnorm(h, ln_mix[i])
        proj = u @ w_in[i]
        x_lru, g_lru, q, k, v = jnp.split(proj, split_at, axis=-1)
        xc = causal_dwconv(x_lru, conv_w[i], conv_b[i])
        y_lru = rglru(xc, gate_a_w[i], gate_a_b[i], gate_x_w[i], gate_x_b[i], lru_lambda[i])
        y_lru = y_lru * jax.nn.gelu(g_lru)
        q = rmsnorm(q.reshape(B, T, N_HEADS, HEAD_DIM), q_gain[i])
        k = rmsnorm(k.reshape(B, T, N_HEADS, HEAD_DIM), k_gain[i])
        v = v.reshape(B, T, N_HEADS, HEAD_DIM)
        y_att = moba_attention(q, k, v, slopes)
        h = h + jnp.concatenate([y_lru, y_att], axis=-1) @ w_out[i]
        u = rmsnorm(h, ln_ffn[i])
        g_up, v_up = jnp.split(u @ w_up[i], 2, axis=-1)
        g_up = causal_dwconv(g_up, ffn_conv_w[i], ffn_conv_b[i])
        h = h + (jax.nn.gelu(g_up) * v_up) @ w_down[i]
        gate = jax.nn.sigmoid(rmsnorm(h, ln_ple[i]) @ w_ple_gate[i])
        h = h + gate * (p[i].astype(h.dtype) @ w_ple_proj[i])
    return h


_drawn_inputs = setup_inputs


def setup_inputs(seed=0):
    import zlib

    import numpy as np

    out = dict(_drawn_inputs(seed))
    spreads = {}
    factors = {'gate_a_b': 64.0,
     'gate_x_b': 60.922,
     'q_gain': 6.474,
     'k_gain': 7.162,
     'ffn_conv_b': 8.0,
     'ln_ple': 7.356,
     'conv_b': 2.798}
    for name, (base, spread) in spreads.items():
        noise = np.random.default_rng([zlib.crc32(name.encode()), seed]).standard_normal(out[name].shape)
        drawn = base * np.exp(spread * noise) if base else spread * noise
        out[name] = __import__('jax').numpy.asarray(drawn.astype(out[name].dtype))
    for name, factor in factors.items():
        out[name] = (out[name] * factor).astype(out[name].dtype)
    return out
```

```python
from contextlib import ExitStack

import concourse.bass as bass
from concourse import mybir

F32 = mybir.dt.float32
F32R = mybir.dt.float32r
I32 = mybir.dt.int32
ALU = mybir.AluOpType
ACT = mybir.ActivationFunctionType
AX = mybir.AxisListType

P = 128
T = 512
TT = T // P
D = 1024
KD = D // P
LRU = 512
LT = LRU // P
HEADS = 8
DH = 64
PAIRS = HEADS // 2
FF = 3072
FT = FF // P
PLE = 256
EPS = 1e-6
NEG = -1e30
RING = 4
CW = 1024
KB = 1024

C_XL = 0
C_GL = C_XL + LT
C_Q = C_GL + LT
C_K = C_Q + 4
C_V = C_K + 4
C_OL = C_V + 4
C_OA = C_OL + 4
C_UP = C_OA + 4
C_DN = C_UP + 2 * FT
C_PP = C_DN + 3 * KD
C_PG = C_PP + 2
N_CHUNKS = C_PG + 8

V_LN_MIX, V_CONV_W, V_CONV_B, V_BA, V_BX, V_LAM = 0, 8, 24, 28, 32, 36
V_LN_FFN, V_LN_PLE, V_QG, V_KG, NA = 40, 48, 56, 57, 58
V_FCW, V_FCB, NB = 58, 58 + 3 * FT, 4 * FT
NV = NA + NB

SCORES = [(3, 0, 0), (2, 1, 0), (0, 1, 384), (1, 2, 0)]
S_OFF = {3: 0, 2: 512, 0: 896, 1: 1024}
PT_OFF = {0: 0, 1: 512, 3: 896, 2: 1024}
S_COLS = 1280


def build(nc, x, p, ln_mix, w_in, conv_w, conv_b, gate_a_w, gate_a_b, gate_x_w, gate_x_b, lru_lambda,
          q_gain, k_gain, w_out, ln_ffn, w_up, ffn_conv_w, ffn_conv_b, w_down, ln_ple, w_ple_gate,
          w_ple_proj, out):
    with ExitStack() as ctx:
        arena = 203 * KB
        base = [nc.sbuf_base + 31 & ~31]

        def at(name, shape, offset, dt=F32):
            return nc.alloc_sbuf_tensor_at(name, shape, dt, offset=base[0] + offset)

        def sem(name):
            return ctx.enter_context(nc.semaphore(name))

        raw = [at(f"raw{s}", [P, CW], 4 * KB * s) for s in range(RING)]
        whi = [at(f"whi{s}", [P, CW], 4 * KB * (4 + s), F32R) for s in range(RING)]
        wlo = [at(f"wlo{s}", [P, CW], 4 * KB * (8 + s), F32R) for s in range(RING)]
        res = at("res", [P, KD, T], 48 * KB)
        uhi = at("uhi", [P, KD, T], 64 * KB, F32R)
        ulo = at("ulo", [P, KD, T], 80 * KB, F32R)
        BIG = 96 * KB
        xtok = at("xtok", [P, TT, D], BIG)
        lx = at("lx", [P, LT, T], BIG)
        lt = at("lt", [P, LT, T], BIG + 8 * KB)
        mixhi = at("mixhi", [P, KD, T], BIG + 16 * KB, F32R)
        mixlo = at("mixlo", [P, KD, T], BIG + 32 * KB, F32R)
        li = at("li", [P, LT, T], BIG + 24 * KB)
        lq = at("lq", [P, LT, T], BIG + 40 * KB)
        qk_tok = [at("qtok", [P, TT, T], BIG + 48 * KB), at("ktok", [P, TT, T], BIG + 56 * KB)]
        prob = [at(f"prob{i}", [P, S_COLS], BIG + (48 + 5 * i) * KB) for i in range(2)]
        prT = [at(f"prT{i}", [P, S_COLS], BIG + (58 + 5 * i) * KB) for i in range(2)]
        vtok = at("vtok", [P, TT, T], BIG + 68 * KB)
        lg = at("lg", [P, LT, T], BIG + 68 * KB)
        qkT = [at("qT", [P, PAIRS, T], BIG + 76 * KB), at("kT", [P, PAIRS, T], BIG + 84 * KB)]
        gw = at("gw", [P, 2, LT, P], BIG + 92 * KB)
        acthi = at("acthi", [P, FT, T], BIG, F32R)
        actlo = at("actlo", [P, FT, T], BIG + 48 * KB, F32R)
        pThi = at("pThi", [P, 2, T], BIG, F32R)
        pTlo = at("pTlo", [P, 2, T], BIG + 4 * KB, F32R)
        htok = at("htok", [P, TT, D], BIG + 8 * KB)
        pp = at("pp", [P, TT, D], BIG + 24 * KB)
        pT = at("pT", [P, 2, T], BIG + 72 * KB)
        sg = at("sg", [P, TT, D], BIG + 40 * KB)
        fin = at("fin", [P, TT, D], BIG + 56 * KB)
        TMP = 192 * KB
        tmp = at("tmp", [P, 4, T], TMP)
        slope_r = [at(f"slope_r{i}", [P, T], TMP + 2 * KB * i) for i in range(2)]
        ptok = at("ptok", [P, TT, PLE], TMP)
        iota = at("iota", [P, T], TMP, I32)
        rbc = at("rbc", [P, T], 200 * KB)
        dist = at("dist", [P, T], 202 * KB)
        acc = at("acc", [P, T], 202 * KB)
        C0 = 204 * KB
        ident = at("ident", [P, P], C0)
        ones = at("ones", [P, P], C0 + 512)
        vec = at("vec", [P, NV], C0 + 1024)
        sp4 = at("sp4", [P, LT], C0 + 1664)
        small = at("small", [P, 48], C0 + 1696)
        ssq = at("ssq", [P, 2, TT * HEADS], C0 + 1888)
        sm = at("sm", [P, 2, 16], C0 + 2144)
        stage_a = at("stage_a", [NA, P], TMP)
        stage_b = at("stage_b", [NB, P], TMP + 512)
        junk = at("junk", [P, D], TMP + 2 * KB)
        ss1, rstd1, ss3, rstd3 = (small[:, 4 * i:4 * i + 4] for i in range(4))
        z4, az4, e4, w4, s4, q4, h4 = (small[:, 16 + 4 * i:20 + 4 * i] for i in range(7))
        assert C0 + 2144 + 128 <= 207 * KB

        bank = [ctx.enter_context(nc.psum_tensor(f"bank{i}", [P, 512], F32)) for i in range(8)]

        raw_in = [sem(f"raw_in{s}") for s in range(RING)]
        w_hi, w_lo = sem("w_hi"), sem("w_lo")
        chunk_done = sem("chunk_done")
        x_in = [sem(f"x_in{j}") for j in range(TT)]
        stage_in, gw_in, p_in = sem("stage_in"), sem("gw_in"), sem("p_in")
        ident_ok, gw_zero, dist_ok, pool_step = sem("ident_ok"), sem("gw_zero"), sem("dist_ok"), sem("pool_step")
        vec_t, vec_ok, sp_step, sp_ok = sem("vec_t"), sem("vec_ok"), sem("sp_step"), sem("sp_ok")
        exp_lam = sem("exp_lam")
        xt_done, res_ok, u_hi, u_lo = sem("xt_done"), sem("res_ok"), sem("u_hi"), sem("u_lo")
        ss_step, ms_ok, std_ok, rstd_ok = sem("ss_step"), sem("ms_ok"), sem("std_ok"), sem("rstd_ok")
        diag_ok, bc_done, rbc_ok = sem("diag_ok"), sem("bc_done"), sem("rbc_ok")
        xs_ok, tap_ok, conv_step, gs_ok, gelu_ok = (sem(n) for n in ("xs_ok", "tap_ok", "conv_step", "gs_ok", "gelu_ok"))
        gates_done, r_ok, i_ok, tanh_ok, sqrt_ok = (sem(n) for n in ("gates_done", "r_ok", "i_ok", "tanh_ok", "sqrt_ok"))
        den_ok, lru_step, y_ok, y_hi, y_lo = (sem(n) for n in ("den_ok", "lru_step", "y_ok", "y_hi", "y_lo"))
        tok_ok, sq_ok, red_ok, qk_step, qk_ms, qk_std, qk_norm_ok = (
            sem(n) for n in ("tok_ok", "sq_ok", "red_ok", "qk_step", "qk_ms", "qk_std", "qk_norm_ok"))
        qk_t, qkT_ok, v_ok = sem("qk_t"), sem("qkT_ok"), sem("v_ok")
        s_done, slope_ok, logit_ok, nmax_ok, exp_ok, rinv_ok, prob_ok = (
            sem(n) for n in ("s_done", "slope_ok", "logit_ok", "nmax_ok", "exp_ok", "rinv_ok", "prob_ok"))
        pt_done, prT_ok, pv_done, att_hi, att_lo = (sem(n) for n in ("pt_done", "prT_ok", "pv_done", "att_hi", "att_lo"))
        fill_done = sem("fill_done")
        part_ok = sem("part_ok")
        res_add = sem("res_add")
        sqr, acc_ok, sos_done = sem("sqr"), sem("acc_ok"), sem("sos_done")
        g_out, f_tap, f_conv, f_gelu, v_out, f_prod, act_hi, act_lo = (
            sem(n) for n in ("g_out", "f_tap", "f_conv", "f_gelu", "v_out", "f_prod", "act_hi", "act_lo"))
        p_t, pT_ok, p_hi, p_lo, ht_done, ht_ok, pp_ok = (
            sem(n) for n in ("p_t", "pT_ok", "p_hi", "p_lo", "ht_done", "ht_ok", "pp_ok"))
        gate_row, sig_ok, mul_ok, fin_ok, out_done = (sem(n) for n in ("gate_row", "sig_ok", "mul_ok", "fin_ok", "out_done"))

        block = ctx.enter_context(nc.Block())

        @block.sync
        def _(sp):
            for j in range(TT):
                sp.dma_start(xtok[:, j, :], x[j * P:(j + 1) * P, :]).then_inc(x_in[j], 16)

            def load(c, s, src, shape, first=False):
                if not first:
                    sp.wait_ge(w_lo, c - (RING - 1))
                dst = raw[s][:, :].rearrange("p (k n) -> p k n", k=shape)
                sp.dma_start(dst, src).then_inc(raw_in[s], 16)

            def tile_of(w, r0, nk, c0, nc_):
                return w[r0:r0 + nk * P, bass.ds(c0, nc_)].rearrange("(k p) n -> p k n", p=P)

            for m in range(2 * LT):
                load(C_XL + m, m % RING, tile_of(w_in, 0, KD, m * P, P), KD, first=m < RING)
            with sp.Fori(0, 3) as t:
                for s in range(4):
                    load(C_Q + s + t * 4, s, tile_of(w_in, 2 * s * P, 2, t * T + 2 * LRU, T), 2)
            for part in range(2):
                for s in range(4):
                    load(C_OL + 4 * part + s, s, tile_of(w_out, part * LRU, LT, s * 2 * P, 2 * P), LT)
            with sp.Fori(0, FT // 2) as i:
                for t in range(2):
                    for half in range(2):
                        load(C_UP + 2 * t + half + i * 4, 2 * t + half,
                             tile_of(w_up, 0, KD, i * (2 * P) + (half * FF + t * P), P), KD)
            with sp.Fori(0, 2) as i:
                for m in range(4):
                    for s in range(3):
                        load(C_DN + 3 * m + s + i * 12, (3 * m + s) % RING,
                             tile_of(w_down, s * D, KD, i * (4 * P) + m * P, P), KD)
            sp.wait_ge(act_lo, FT)
            sp.dma_start(ptok[:, :, :], p.rearrange("(j p) n -> p j n", p=P)).then_inc(p_in, 16)
            for n in range(2):
                load(C_PP + n, n, tile_of(w_ple_proj, 0, 2, n * T, T), 2)
            for n in range(2):
                for s in range(4):
                    load(C_PG + 4 * n + s, (C_PG + s) % RING, tile_of(w_ple_gate, 2 * s * P, 2, n * T, T), 2)
            for n in range(2):
                for j in range(TT):
                    sp.wait_ge(fin_ok, 4 * n + j + 1)
                    sp.dma_start(out[j * P:(j + 1) * P, n * T:(n + 1) * T], fin[:, j, n * T:(n + 1) * T]).then_inc(out_done, 16)
            sp.wait_ge(out_done, 16 * 2 * TT)

        @block.gpsimd
        def _(pool):
            nc.gpsimd.memset(ident[:, :], 0.0).then_inc(pool_step, 1)
            pool.wait_ge(pool_step, 1)
            nc.gpsimd.affine_select(out=ident[:, :], in_=ident[:, :], compare_op=ALU.not_equal, fill=1.0, base=0,
                                    pattern=[[-1, P]], channel_multiplier=1).then_inc(ident_ok, 1)
            nc.gpsimd.memset(gw[:, :, :, :], 0.0).then_inc(gw_zero, 1)
            nc.gpsimd.memset(ones[:, :], 1.0).then_inc(ident_ok, 1)

            def lo_part(c, s):
                pool.wait_ge(w_hi, c + 1)
                nc.gpsimd.tensor_tensor(wlo[s][:, :], raw[s][:, :], whi[s][:, :].bitcast(F32), ALU.subtract).then_inc(w_lo, 1)

            for c in range(RING):
                lo_part(c, c)
            pool.wait_ge(vec_ok, 2)
            pool.wait_ge(ss_step, TT)
            nc.gpsimd.iota(iota[:, :], pattern=[[1, T]], base=-(T - P), channel_multiplier=-1).then_inc(pool_step, 1)
            pool.wait_ge(pool_step, 2)
            nc.gpsimd.tensor_copy(dist[:, :], iota[:, :]).then_inc(pool_step, 1)
            pool.wait_ge(pool_step, 3)
            nc.gpsimd.affine_select(out=dist[:, :], in_=dist[:, :], compare_op=ALU.is_ge, fill=NEG, base=T - P,
                                    pattern=[[-1, T]], channel_multiplier=1).then_inc(dist_ok, 1)
            with pool.Fori(1, N_CHUNKS // RING) as i:
                for s in range(RING):
                    lo_part(s + i * RING, s)
            for c in range(N_CHUNKS // RING * RING, N_CHUNKS):
                lo_part(c, c % RING)

        @block.scalar
        def _(act):
            def rows(dst, r, src, n):
                act.dma_start(dst[r:r + n, :], src.rearrange("(m c) -> m c", c=P)).then_inc(stage_in, 16)

            rows(stage_a, V_LN_MIX, ln_mix, KD)
            act.dma_start(stage_a[V_CONV_W:V_CONV_W + 16, :], conv_w.rearrange("k (m c) -> (k m) c", c=P)).then_inc(stage_in, 16)
            rows(stage_a, V_CONV_B, conv_b, LT)
            rows(stage_a, V_BA, gate_a_b, LT)
            rows(stage_a, V_BX, gate_x_b, LT)
            rows(stage_a, V_LAM, lru_lambda, LT)
            rows(stage_a, V_LN_FFN, ln_ffn, KD)
            rows(stage_a, V_LN_PLE, ln_ple, KD)
            for half in range(2):
                cols = slice(half * DH, (half + 1) * DH)
                act.dma_start(stage_a[V_QG:V_QG + 1, cols], q_gain.rearrange("(o d) -> o d", o=1)).then_inc(stage_in, 16)
                act.dma_start(stage_a[V_KG:V_KG + 1, cols], k_gain.rearrange("(o d) -> o d", o=1)).then_inc(stage_in, 16)
            act.dma_start(stage_b[0:3 * FT, :], ffn_conv_w.rearrange("k (m c) -> (k m) c", c=P)).then_inc(stage_in, 16)
            rows(stage_b, 3 * FT, ffn_conv_b, FT)
            act.wait_ge(gw_zero, 1)
            for g, w in enumerate((gate_a_w, gate_x_w)):
                blocks = w.rearrange("(m two) c d -> two c m d", two=2)
                for half in range(2):
                    act.dma_start(gw[half * DH:(half + 1) * DH, g, :, half * DH:(half + 1) * DH], blocks[half]).then_inc(gw_in, 16)

            def hi_part(c, s, use_done=True):
                act.wait_ge(raw_in[s], 16 + (c - s) * (16 // RING) if not isinstance(c, int) else 16 * (c // RING + 1))
                if use_done:
                    act.wait_ge(chunk_done, c - (RING - 1))
                nc.scalar.activation(whi[s][:, :], raw[s][:, :], ACT.Copy).then_inc(w_hi, 1)

            act.wait_ge(sp_step, 1)
            nc.scalar.activation(e4, az4, ACT.Exp, scale=-1.0).then_inc(exp_lam, 1)
            act.wait_ge(vec_ok, 2)
            for c in range(KD):
                act.wait_ge(xt_done, c + 1)
                nc.scalar.activation(res[:, c, :], bank[c][:, :], ACT.Copy).then_inc(res_ok, 1)
                act.wait_ge(res_ok, c + 1)
                nc.scalar.activation(uhi[:, c, :], res[:, c, :], ACT.Copy, scale=vec[:, V_LN_MIX + c:V_LN_MIX + c + 1]).then_inc(u_hi, 1)
                if c in (3, 5):
                    hi_part((c - 3) // 2, (c - 3) // 2, use_done=False)
            hi_part(2, 2, use_done=False)
            hi_part(3, 3, use_done=False)
            act.wait_ge(ms_ok, 1)
            nc.scalar.activation(rstd1, ss1, ACT.Sqrt).then_inc(std_ok, 1)

            for m in range(LT):
                act.wait_ge(xs_ok, m + 1)
                nc.scalar.activation(lx[:, m, :], lq[:, m, :], ACT.Identity,
                                     bias=vec[:, V_CONV_B + m:V_CONV_B + m + 1],
                                     scale=vec[:, V_CONV_W + 3 * LT + m:V_CONV_W + 3 * LT + m + 1]).then_inc(tap_ok, 1)
                hi_part(4 + m, m)
            for m in range(LT):
                hi_part(8 + m, m)
            for m in range(LT):
                act.wait_ge(gs_ok, m + 1)
                nc.scalar.activation(lg[:, m, :], lg[:, m, :], ACT.Gelu_apprx_tanh).then_inc(gelu_ok, 1)
            act.wait_ge(sp_ok, 1)
            for m in range(LT):
                hi_part(12 + m, m)
                act.wait_ge(gates_done, m + 1)
                b = 2 * (m % 2)
                nc.scalar.activation(lt[:, m, :], bank[b][:, :], ACT.Sigmoid, bias=vec[:, V_BA + m:V_BA + m + 1]).then_inc(r_ok, 1)
                nc.scalar.activation(li[:, m, :], bank[b + 1][:, :], ACT.Sigmoid, bias=vec[:, V_BX + m:V_BX + m + 1]).then_inc(i_ok, 1)
                act.wait_ge(r_ok, m + 1)
                nc.scalar.activation(lt[:, m, :], lt[:, m, :], ACT.Tanh, scale=sp4[:, m:m + 1]).then_inc(tanh_ok, 1)

            def qk_squares(w):
                for j in range(TT):
                    act.wait_ge(tok_ok, TT * w + j + 1)
                    if w:
                        act.wait_ge(red_ok, j + 1)
                    nc.scalar.activation(tmp[:, j, :], qk_tok[w][:, j, :], ACT.Square).then_inc(sq_ok, 1)

            def qk_sqrt(w):
                act.wait_ge(qk_ms, w + 1)
                nc.scalar.activation(ssq[:, w, :], ssq[:, w, :], ACT.Sqrt).then_inc(qk_std, 1)

            def qk_turned(w):
                for r in range(PAIRS):
                    act.wait_ge(qk_t, PAIRS * w + r + 1)
                    nc.scalar.activation(qkT[w][:, r, :], bank[(4 if w == 0 else 0) + r][:, :], ACT.Copy,
                                         scale=vec[:, V_QG + w:V_QG + w + 1]).then_inc(qkT_ok, 1)

            qk_squares(0)
            for m in range(LT):
                act.wait_ge(den_ok, m + 1)
                nc.scalar.activation(lt[:, m, :], lt[:, m, :], ACT.Sqrt).then_inc(sqrt_ok, 1)
            qk_sqrt(0)
            hi_part(16, 0)
            hi_part(17, 1)
            qk_turned(0)
            hi_part(18, 2)
            hi_part(19, 3)
            qk_squares(1)
            qk_sqrt(1)
            for m in range(LT):
                act.wait_ge(y_ok, m + 1)
                nc.scalar.activation(mixhi[:, m, :], lq[:, m, :], ACT.Copy).then_inc(y_hi, 1)
            hi_part(20, 0)
            hi_part(21, 1)
            qk_turned(1)
            hi_part(22, 2)
            hi_part(23, 3)

            def exps(h):
                act.wait_ge(nmax_ok, h + 1)
                for i, _, _ in SCORES:
                    v = prob[h % 2][:, S_OFF[i]:S_OFF[i] + (i + 1) * P]
                    nc.scalar.activation(v, v, ACT.Exp, bias=sm[:, h % 2, 4 + i:5 + i],
                                         accum_out=sm[:, h % 2, 8 + i:9 + i]).then_inc(exp_ok, 1)

            for j in range(TT):
                act.wait_ge(chunk_done, C_V + 4)
                if j == 0:
                    act.wait_ge(y_lo, LT)
                nc.scalar.activation(vtok[:, j, :], bank[4 + j][:, :], ACT.Copy, scale=rstd1[:, j:j + 1]).then_inc(v_ok, 1)
            exps(0)
            for h in range(HEADS):
                for part, b in ((0, 3), (1, 4), (2, 3)):
                    act.wait_ge(pt_done, 3 * h + part + 1)
                    if h >= 2 and part == 0:
                        act.wait_ge(pv_done, h - 1)
                    w = 512 if part < 2 else 256
                    nc.scalar.activation(prT[h % 2][:, 512 * part:512 * part + w], bank[b][:, 0:w], ACT.Copy).then_inc(prT_ok, 1)
                if h + 1 < HEADS:
                    exps(h + 1)
                if h % 2 == 1:
                    act.wait_ge(pv_done, h + 1)
                    nc.scalar.activation(mixhi[:, LT + h // 2, :], bank[5][:, :], ACT.Copy).then_inc(att_hi, 1)
                    hi_part(24 + h // 2, h // 2)

            def norm_split(m, n, gain):
                act.wait_ge(res_add, n + 1)
                nc.scalar.activation(uhi[:, m, :], res[:, m, :], ACT.Copy, scale=vec[:, bass.ds(m + gain, 1)]).then_inc(u_hi, 1)
                if not isinstance(n, int) or n >= 2:
                    act.wait_ge(acc_ok, n - 1)
                nc.scalar.activation(tmp[:, 2 + (m % 2 if isinstance(m, int) else 0), :], res[:, m, :], ACT.Square).then_inc(sqr, 1)

            for m in range(KD):
                norm_split(m, m, V_LN_FFN)
                if m % 2 == 1:
                    hi_part(C_UP + m // 2, m // 2)
            act.wait_ge(ms_ok, 2)
            nc.scalar.activation(rbc[:, :], rbc[:, :], ACT.Sqrt).then_inc(std_ok, 1)

            def mlp(it):
                for t in range(2):
                    f = it * 2 + t
                    c = it * 4 + (C_UP + 2 * t)
                    hi_part(c + RING, 2 * t)
                    act.wait_ge(g_out, f + 1)
                    act.wait_ge(vec_ok, 3)
                    nc.scalar.activation(tmp[:, 2 + t, :], tmp[:, t, :], ACT.Identity, bias=0.0,
                                         scale=vec[:, bass.ds(f + (V_FCW + 2 * FT), 1)]).then_inc(f_tap, 1)
                    hi_part(c + RING + 1, 2 * t + 1)
                    act.wait_ge(f_conv, f * 2 + 2)
                    act.wait_ge(vec_ok, 3)
                    nc.scalar.activation(tmp[:, 2 + t, :], tmp[:, 2 + t, :], ACT.Gelu_apprx_tanh,
                                         bias=vec[:, bass.ds(f + V_FCB, 1)]).then_inc(f_gelu, 1)
                    act.wait_ge(f_prod, f + 1)
                    act.wait_ge(chunk_done, C_UP)
                    nc.scalar.activation(acthi[:, f, :], tmp[:, 2 + t, :], ACT.Copy).then_inc(act_hi, 1)

            with act.Fori(0, FT // 2) as it:
                mlp(it)
            with act.Fori(0, 2) as i:
                for m in range(4):
                    for s in range(3):
                        hi_part(i * 12 + (C_DN + RING + 3 * m + s), (3 * m + s) % RING)
                    act.wait_ge(acc_ok, i * 4 + (KD + m - 1))
                    act.wait_ge(res_add, i * 4 + (KD + m + 1))
                    act.wait_ge(vec_ok, 3)
                    nc.scalar.activation(uhi[:, i * 4 + m, :], res[:, i * 4 + m, :], ACT.Copy,
                                         scale=vec[:, bass.ds(i * 4 + (V_LN_PLE + m), 1)]).then_inc(u_hi, 1)
                    nc.scalar.activation(tmp[:, 2 + m % 2, :], res[:, i * 4 + m, :], ACT.Square).then_inc(sqr, 1)

            for k in range(2):
                act.wait_ge(pT_ok, k + 1)
                nc.scalar.activation(pThi[:, k, :], pT[:, k, :], ACT.Copy).then_inc(p_hi, 1)
            for n in range(2):
                for j in range(TT):
                    act.wait_ge(ht_done, 4 * n + j + 1)
                    nc.scalar.activation(htok[:, j, n * T:(n + 1) * T], bank[2 + j % 2][:, :], ACT.Copy).then_inc(ht_ok, 1)
            act.wait_ge(ms_ok, 3)
            nc.scalar.activation(rstd3, ss3, ACT.Sqrt).then_inc(std_ok, 1)
            hi_part(C_PG + 2, C_PP % RING)
            for n in range(2):
                act.wait_ge(chunk_done, C_PP + n + 1)
                if n == 1:
                    hi_part(C_PG + 3, (C_PP + 1) % RING)
                for j in range(TT):
                    nc.scalar.activation(pp[:, j, n * T:(n + 1) * T], bank[(4 if n == 0 else 0) + j][:, :], ACT.Copy).then_inc(pp_ok, 1)
            act.wait_ge(rstd_ok, 2)
            for n in range(2):
                for s in range(4):
                    c = C_PG + 4 * n + s + RING
                    if C_PG + 4 <= c < N_CHUNKS:
                        hi_part(c, c % RING)
                for j in range(TT):
                    act.wait_ge(gate_row, 4 * n + j + 1)
                    nc.scalar.activation(sg[:, j, n * T:(n + 1) * T], bank[(4 if n == 0 else 0) + j][:, :], ACT.Sigmoid,
                                         scale=rstd3[:, j:j + 1]).then_inc(sig_ok, 1)

        @block.vector
        def _(dve):
            V = nc.vector
            dve.wait_ge(vec_t, 2)
            V.tensor_copy(vec[:, 0:NA], bank[7][:, 0:NA]).then_inc(vec_ok, 1)
            V.tensor_copy(vec[:, NA:NV], bank[6][:, 0:NB]).then_inc(vec_ok, 1)
            dve.wait_ge(vec_ok, 2)
            lam = vec[:, V_LAM:V_LAM + LT]
            V.scalar_tensor_tensor(az4, lam, -1.0, lam, ALU.mult, ALU.max).then_inc(sp_step, 1)
            for j in range(TT):
                dve.wait_ge(x_in[j], 16)
                if j:
                    dve.wait_ge(ss_step, j)
                V.tensor_tensor_reduce(junk[:, :], xtok[:, j, :], xtok[:, j, :], 1.0, 0.0, ALU.mult, ALU.add,
                                       ss1[:, j:j + 1]).then_inc(ss_step, 1)
            dve.wait_ge(ss_step, TT)
            V.tensor_scalar(ss1, ss1, 1.0 / D, EPS, ALU.mult, ALU.add).then_inc(ms_ok, 1)
            V.tensor_scalar(vec[:, V_QG:V_QG + 1], vec[:, V_QG:V_QG + 1], float(DH) ** -0.5, None, ALU.mult).then_inc(vec_ok, 1)

            def split_u(m, n, gain):
                dve.wait_ge(u_hi, n + 1)
                V.scalar_tensor_tensor(ulo[:, m, :], res[:, m, :], vec[:, bass.ds(m + gain, 1)], uhi[:, m, :].bitcast(F32),
                                       ALU.mult, ALU.subtract).then_inc(u_lo, 1)

            for c in range(KD):
                split_u(c, c, V_LN_MIX)
            dve.wait_ge(std_ok, 1)
            V.reciprocal(rstd1, rstd1).then_inc(rstd_ok, 1)
            dve.wait_ge(rstd_ok, 1)
            for j in range(TT):
                V.tensor_scalar(tmp[:, 3, j * P:(j + 1) * P], ident[:, :], rstd1[:, j:j + 1], None, ALU.mult).then_inc(diag_ok, 1)
            steps = [1]

            def step(ins):
                ins.then_inc(sp_step, 1)
                steps[0] += 1
                dve.wait_ge(sp_step, steps[0])

            dve.wait_ge(exp_lam, 1)
            step(V.tensor_scalar(w4, e4, 2.0, None, ALU.add))
            step(V.reciprocal(w4, w4))
            step(V.tensor_tensor(s4, e4, w4, ALU.mult))
            step(V.tensor_tensor(q4, s4, s4, ALU.mult))
            step(V.tensor_scalar(h4, q4, 1.0 / 17, None, ALU.mult))
            for k in range(15, 1, -2):
                step(V.scalar_tensor_tensor(h4, h4, 1.0 / k, q4, ALU.add, ALU.mult))
            step(V.scalar_tensor_tensor(h4, h4, 1.0, s4, ALU.add, ALU.mult))
            step(V.tensor_scalar(z4, lam, -1.0, 0.0, ALU.mult, ALU.max))
            step(V.scalar_tensor_tensor(z4, h4, 2.0, z4, ALU.mult, ALU.add))
            V.tensor_scalar(sp4[:, :], z4, 4.0, None, ALU.mult).then_inc(sp_ok, 1)

            dve.wait_ge(bc_done, 1)
            V.tensor_copy(rbc[:, :], bank[4][:, :]).then_inc(rbc_ok, 1)
            dve.wait_ge(rbc_ok, 1)

            def conv(m):
                dve.wait_ge(tap_ok, m + 1)
                for k in range(1, 4):
                    w = V_CONV_W + (3 - k) * LT + m
                    V.scalar_tensor_tensor(lx[:, m, k:T], lq[:, m, 0:T - k], vec[:, w:w + 1], lx[:, m, k:T],
                                           ALU.mult, ALU.add).then_inc(conv_step, 1)
                    dve.wait_ge(conv_step, 3 * m + k)

            for m in range(LT):
                dve.wait_ge(chunk_done, C_XL + m + 1)
                V.tensor_tensor(lq[:, m, :], bank[m % 2][:, :], rbc[:, :], ALU.mult).then_inc(xs_ok, 1)
                conv(m)
            for m in range(LT):
                dve.wait_ge(chunk_done, C_GL + m + 1)
                V.tensor_tensor(lg[:, m, :], bank[2 + m % 2][:, :], rbc[:, :], ALU.mult).then_inc(gs_ok, 1)

            n_step = [0]

            def lru_next(ins):
                ins.then_inc(lru_step, 1)
                n_step[0] += 1
                dve.wait_ge(lru_step, n_step[0])

            def den(m):
                dve.wait_ge(tanh_ok, m + 1)
                V.tensor_scalar(lq[:, m, :], lt[:, m, :], 1.0, None, ALU.add).then_inc(den_ok, 1)
                dve.wait_ge(den_ok, m + 1)
                lru_next(V.reciprocal(lq[:, m, :], lq[:, m, :]))
                lru_next(V.tensor_tensor(li[:, m, :], li[:, m, :], lx[:, m, :], ALU.mult))
                lru_next(V.tensor_scalar(lx[:, m, :], lq[:, m, :], 2.0, -1.0, ALU.mult, ALU.add))

            def scan(m):
                dve.wait_ge(sqrt_ok, m + 1)
                lru_next(V.scalar_tensor_tensor(lt[:, m, :], lt[:, m, :], 2.0, lq[:, m, :], ALU.mult, ALU.mult))
                lru_next(V.memset(lt[:, m, 0:1], 1.0))
                lru_next(V.tensor_tensor(li[:, m, :], li[:, m, :], lt[:, m, :], ALU.mult))
                lru_next(V.tensor_tensor_scan(lt[:, m, :], lx[:, m, :], li[:, m, :], 0.0, ALU.mult, ALU.add))
                dve.wait_ge(gelu_ok, m + 1)
                V.tensor_tensor(lq[:, m, :], lt[:, m, :], lg[:, m, :], ALU.mult).then_inc(y_ok, 1)

            def y_split(m):
                dve.wait_ge(y_hi, m + 1)
                V.tensor_tensor(mixlo[:, m, :], lq[:, m, :], mixhi[:, m, :].bitcast(F32), ALU.subtract).then_inc(y_lo, 1)

            def tok_out(w):
                dve.wait_ge(chunk_done, C_Q + 4 * (w + 1))
                for j in range(TT):
                    V.tensor_scalar(qk_tok[w][:, j, :], bank[(4 if w == 0 else 0) + j][:, :], rstd1[:, j:j + 1], None,
                                    ALU.mult).then_inc(tok_ok, 1)

            def qk_sums(w):
                for j in range(TT):
                    dve.wait_ge(sq_ok, TT * w + j + 1)
                    V.tensor_reduce(ssq[:, w, j * HEADS:(j + 1) * HEADS], tmp[:, j, :].rearrange("p (h d) -> p h d", d=DH),
                                    AX.X, ALU.add).then_inc(red_ok, 1)
                dve.wait_ge(red_ok, TT * (w + 1))
                V.tensor_scalar(ssq[:, w, :], ssq[:, w, :], 1.0 / DH, EPS, ALU.mult, ALU.add).then_inc(qk_ms, 1)

            def qk_scale(w):
                dve.wait_ge(qk_std, w + 1)
                V.reciprocal(ssq[:, w, :], ssq[:, w, :]).then_inc(qk_step, 1)
                dve.wait_ge(qk_step, w + 1)
                for j in range(TT):
                    v = qk_tok[w][:, j, :].rearrange("p (h d) -> p h d", d=DH)
                    r = ssq[:, w, j * HEADS:(j + 1) * HEADS].unsqueeze(2).to_broadcast([P, HEADS, DH])
                    V.tensor_tensor(v, v, r, ALU.mult).then_inc(qk_norm_ok, 1)

            for m in range(LT):
                den(m)
            tok_out(0)
            qk_sums(0)
            scan(0)
            scan(1)
            qk_scale(0)
            scan(2)
            scan(3)
            tok_out(1)
            qk_sums(1)
            qk_scale(1)
            for m in range(LT):
                y_split(m)

            def logits(h):
                slope = 2.0 ** (-8.0 * (h + 1) / HEADS)
                if h == 0:
                    dve.wait_ge(dist_ok, 1)
                    dve.wait_ge(qk_norm_ok, 2 * TT)
                if h >= 2:
                    dve.wait_ge(logit_ok, 4 * (h - 1))
                V.tensor_scalar(slope_r[h % 2][:, :], dist[:, :], slope, None, ALU.mult).then_inc(slope_ok, 1)
                dve.wait_ge(slope_ok, h + 1)
                dve.wait_ge(s_done, h + 1)
                if h >= 2:
                    dve.wait_ge(pt_done, 3 * (h - 1))
                for i, b, c0 in SCORES:
                    w = (i + 1) * P
                    V.tensor_tensor_reduce(prob[h % 2][:, S_OFF[i]:S_OFF[i] + w], bank[b][:, c0:c0 + w],
                                           slope_r[h % 2][:, (TT - 1 - i) * P:T], 1.0, 3.0 * NEG, ALU.add, ALU.max,
                                           sm[:, h % 2, i:i + 1]).then_inc(logit_ok, 1)
                dve.wait_ge(logit_ok, 4 * (h + 1))
                V.tensor_scalar(sm[:, h % 2, 4:8], sm[:, h % 2, 0:4], -1.0, None, ALU.mult).then_inc(nmax_ok, 1)

            def normalise(h):
                dve.wait_ge(exp_ok, 4 * (h + 1))
                V.reciprocal(sm[:, h % 2, 12:16], sm[:, h % 2, 8:12]).then_inc(rinv_ok, 1)
                dve.wait_ge(rinv_ok, h + 1)
                for i, _, _ in SCORES:
                    v = prob[h % 2][:, S_OFF[i]:S_OFF[i] + (i + 1) * P]
                    V.tensor_scalar(v, v, sm[:, h % 2, 12 + i:13 + i], None, ALU.mult).then_inc(prob_ok, 1)

            logits(0)
            normalise(0)
            for h in range(HEADS):
                if h + 1 < HEADS:
                    logits(h + 1)
                dve.wait_ge(fill_done, h + 1)
                V.tensor_tensor(res[:, h, :], res[:, h, :], bank[6 + h % 2][:, :], ALU.add).then_inc(part_ok, 1)
                if h + 1 < HEADS:
                    normalise(h + 1)
                if h % 2 == 1:
                    dve.wait_ge(att_hi, h // 2 + 1)
                    V.tensor_tensor(mixlo[:, LT + h // 2, :], bank[5][:, :], mixhi[:, LT + h // 2, :].bitcast(F32),
                                    ALU.subtract).then_inc(att_lo, 1)

            def finish_res(m, n, b, gain, first):
                V.tensor_tensor(res[:, m, :], res[:, m, :], bank[b][:, :], ALU.add).then_inc(res_add, 1)
                split_u(m, n + KD, gain)
                dve.wait_ge(sqr, n + 1)
                sq = tmp[:, 2 + first[1], :]
                if first[0]:
                    V.tensor_copy(acc[:, :], sq).then_inc(acc_ok, 1)
                else:
                    dve.wait_ge(acc_ok, n)
                    V.tensor_tensor(acc[:, :], acc[:, :], sq, ALU.add).then_inc(acc_ok, 1)

            OA_BANK = [6, 7, 0, 1, 2, 3, 4, 5]
            dve.wait_ge(part_ok, KD)
            for m in range(KD):
                if m % 2 == 0:
                    dve.wait_ge(chunk_done, C_OA + m // 2 + 1)
                finish_res(m, m, OA_BANK[m], V_LN_FFN, (m == 0, m % 2))
            dve.wait_ge(sos_done, 1)
            V.tensor_scalar(rbc[:, :], bank[7][:, :], 1.0 / D, EPS, ALU.mult, ALU.add).then_inc(ms_ok, 1)
            dve.wait_ge(std_ok, 2)
            V.reciprocal(rbc[:, :], rbc[:, :]).then_inc(rbc_ok, 1)
            dve.wait_ge(rbc_ok, 2)

            def mlp(it, first):
                for t in range(2):
                    f = it * 2 + t
                    c = it * 4 + (C_UP + 2 * t)
                    g, y = tmp[:, t, :], tmp[:, 2 + t, :]
                    dve.wait_ge(chunk_done, c + 1)
                    if not first:
                        dve.wait_ge(f_prod, f - 1)
                    V.tensor_tensor(g, bank[2 * t][:, :], rbc[:, :], ALU.mult).then_inc(g_out, 1)
                    dve.wait_ge(f_tap, f + 1)
                    for k in range(1, 3):
                        V.scalar_tensor_tensor(y[:, k:T], g[:, 0:T - k], vec[:, bass.ds(f + (V_FCW + (2 - k) * FT), 1)],
                                               y[:, k:T], ALU.mult, ALU.add).then_inc(f_conv, 1)
                        dve.wait_ge(f_conv, f * 2 + k)
                    dve.wait_ge(chunk_done, c + 2)
                    V.tensor_tensor(g, bank[2 * t + 1][:, :], rbc[:, :], ALU.mult).then_inc(v_out, 1)
                    dve.wait_ge(v_out, f + 1)
                    dve.wait_ge(f_gelu, f + 1)
                    V.tensor_tensor(y, g, y, ALU.mult).then_inc(f_prod, 1)
                    dve.wait_ge(act_hi, f + 1)
                    V.tensor_tensor(actlo[:, f, :], y, acthi[:, f, :].bitcast(F32), ALU.subtract).then_inc(act_lo, 1)

            mlp(0, True)
            with dve.Fori(1, FT // 2) as it:
                mlp(it, False)

            def down(i, m, first):
                dve.wait_ge(chunk_done, i * 12 + (C_DN + 3 * m + 3))
                V.tensor_tensor(res[:, i * 4 + m, :], res[:, i * 4 + m, :], bank[4 + m][:, :], ALU.add).then_inc(res_add, 1)
                dve.wait_ge(u_hi, i * 4 + (2 * KD + m + 1))
                V.scalar_tensor_tensor(ulo[:, i * 4 + m, :], res[:, i * 4 + m, :], vec[:, bass.ds(i * 4 + (V_LN_PLE + m), 1)],
                                       uhi[:, i * 4 + m, :].bitcast(F32), ALU.mult, ALU.subtract).then_inc(u_lo, 1)
                dve.wait_ge(sqr, i * 4 + (KD + m + 1))
                dve.wait_ge(acc_ok, i * 4 + (KD + m))
                V.tensor_tensor(acc[:, :], acc[:, :], tmp[:, 2 + m % 2, :], ALU.add).then_inc(acc_ok, 1)

            dve.wait_ge(acc_ok, KD)
            V.memset(acc[:, :], 0.0).then_inc(lru_step, 1)
            dve.wait_ge(lru_step, n_step[0] + 1)
            with dve.Fori(0, 2) as i:
                for m in range(4):
                    down(i, m, False)

            for k in range(2):
                dve.wait_ge(p_t, k + 1)
                V.tensor_copy(pT[:, k, :], bank[k][:, :]).then_inc(pT_ok, 1)
            for k in range(2):
                dve.wait_ge(p_hi, k + 1)
                V.tensor_tensor(pTlo[:, k, :], pT[:, k, :], pThi[:, k, :].bitcast(F32), ALU.subtract).then_inc(p_lo, 1)
            dve.wait_ge(sos_done, 2)
            V.tensor_scalar(ss3, bank[1][:, 0:TT], 1.0 / D, EPS, ALU.mult, ALU.add).then_inc(ms_ok, 1)
            dve.wait_ge(std_ok, 3)
            V.reciprocal(rstd3, rstd3).then_inc(rstd_ok, 1)
            dve.wait_ge(ht_ok, 2 * TT)
            for n in range(2):
                for j in range(TT):
                    s = slice(n * T, (n + 1) * T)
                    k = 4 * n + j + 1
                    dve.wait_ge(sig_ok, k)
                    dve.wait_ge(pp_ok, k)
                    V.tensor_tensor(sg[:, j, s], sg[:, j, s], pp[:, j, s], ALU.mult).then_inc(mul_ok, 1)
                    dve.wait_ge(mul_ok, k)
                    V.tensor_tensor(fin[:, j, s], sg[:, j, s], htok[:, j, s], ALU.add).then_inc(fin_ok, 1)

        @block.tensor
        def _(pe):
            mm = nc.tensor.matmul

            def three(o, ahi, alo, bhi, blo, start, stop):
                mm(o, ahi, bhi, start=start, stop=False)
                mm(o, ahi, blo, start=False, stop=False)
                return mm(o, alo, bhi, start=False, stop=stop)

            def channels(c, s, o, vhi, vlo, k0, n_k, start, stop, before=None):
                pe.wait_ge(w_lo, c + 1)
                for k in range(n_k):
                    if before:
                        before(k)
                    w = slice(k * P, (k + 1) * P)
                    last = three(o, whi[s][:, w], wlo[s][:, w], vhi[:, k0 + k, :], vlo[:, k0 + k, :],
                                 start and k == 0, stop and k == n_k - 1)
                last.then_inc(chunk_done, 1)

            def tokens(c, s, o, vhi, vlo, k0, start, stop, rows=None):
                pe.wait_ge(w_lo, c + 1)
                for j in range(TT):
                    for k in range(2):
                        t, w = slice(j * P, (j + 1) * P), slice(k * T, (k + 1) * T)
                        last = three(o[j][:, :], vhi[:, k0 + k, t], vlo[:, k0 + k, t], whi[s][:, w], wlo[s][:, w],
                                     start and k == 0, stop and k == 1)
                    if rows:
                        last.then_inc(rows, 1)
                    elif j == TT - 1:
                        last.then_inc(chunk_done, 1)

            pe.wait_ge(ident_ok, 2)
            pe.wait_ge(stage_in, 16 * 14)
            nc.tensor.transpose(bank[7][:, 0:NA], stage_a[:, :], ident[0:NA, 0:NA]).then_inc(vec_t, 1)
            nc.tensor.transpose(bank[6][:, 0:NB], stage_b[:, :], ident[0:NB, 0:NB]).then_inc(vec_t, 1)
            for j in range(TT):
                pe.wait_ge(x_in[j], 16)
                for c in range(KD):
                    if j == 0 and c == 6:
                        pe.wait_ge(vec_ok, 2)
                    t = nc.tensor.transpose(bank[c][:, j * P:(j + 1) * P], xtok[:, j, c * P:(c + 1) * P], ident[:, :])
                    if j == TT - 1:
                        t.then_inc(xt_done, 1)

            for m in range(LT):
                if m < 2:
                    pe.wait_ge(res_ok, m + 1)
                else:
                    pe.wait_ge(xs_ok, m - 1)
                channels(C_XL + m, m, bank[m % 2][:, :], uhi, ulo, 0, KD, True, True,
                         before=(lambda k: pe.wait_ge(u_lo, k + 1)) if m == 0 else None)
                if m == 0:
                    pe.wait_ge(diag_ok, TT)
                    pe.wait_ge(res_ok, KD)
                    mm(bank[4][:, :], ones[:, :], tmp[:, 3, :], start=True, stop=True).then_inc(bc_done, 1)
            for m in range(LT):
                if m >= 2:
                    pe.wait_ge(gs_ok, m - 1)
                channels(C_GL + m, m, bank[2 + m % 2][:, :], uhi, ulo, 0, KD, True, True)
            pe.wait_ge(rbc_ok, 1)
            pe.wait_ge(gs_ok, LT)
            pe.wait_ge(gw_in, 64)
            for s in range(4):
                tokens(C_Q + s, s, bank[4:8], uhi, ulo, 2 * s, s == 0, s == 3)
                pe.wait_ge(conv_step, 3 * (s + 1))
                if s >= 2:
                    pe.wait_ge(i_ok, s - 1)
                for g in range(2):
                    last = mm(bank[2 * (s % 2) + g][:, :], gw[:, g, s, :], lx[:, s, :], start=True, stop=True)
                last.then_inc(gates_done, 1)

            def turn(w):
                pe.wait_ge(qk_norm_ok, TT * (w + 1))
                for r in range(PAIRS):
                    for j in range(TT):
                        last = nc.tensor.transpose(bank[(4 if w == 0 else 0) + r][:, j * P:(j + 1) * P],
                                                   qk_tok[w][:, j, r * P:(r + 1) * P], ident[:, :])
                    last.then_inc(qk_t, 1)

            pe.wait_ge(i_ok, LT)
            for s in range(4):
                tokens(C_K + s, s, bank[0:4], uhi, ulo, 2 * s, s == 0, s == 3)
            turn(0)
            pe.wait_ge(qkT_ok, PAIRS)
            for s in range(4):
                tokens(C_V + s, s, bank[4:8], uhi, ulo, 2 * s, s == 0, s == 3)
            turn(1)

            def scores(h):
                pe.wait_ge(qkT_ok, 2 * PAIRS)
                if h:
                    pe.wait_ge(logit_ok, 4 * h)
                r = slice(DH * (h % 2), DH * (h % 2 + 1))
                for i, b, c0 in SCORES:
                    w = (i + 1) * P
                    last = mm(bank[b][:, c0:c0 + w], qkT[0][r, h // 2, i * P:(i + 1) * P], qkT[1][r, h // 2, 0:w],
                              start=True, stop=True)
                last.then_inc(s_done, 1)

            def turn_probs(h):
                pe.wait_ge(prob_ok, 4 * (h + 1))
                for part, b, kts in ((0, 3, (0,)), (1, 4, (1, 3)), (2, 3, (2,))):
                    if part == 2:
                        pe.wait_ge(prT_ok, 3 * h + 1)
                    elif h:
                        pe.wait_ge(prT_ok, 3 * h)
                    for kt in kts:
                        c0 = PT_OFF[kt] - 512 * part
                        for i in range(kt, TT):
                            src = prob[h % 2][:, S_OFF[i] + kt * P:S_OFF[i] + (kt + 1) * P]
                            last = nc.tensor.transpose(bank[b][:, c0 + (i - kt) * P:c0 + (i - kt + 1) * P], src, ident[:, :])
                    last.then_inc(pt_done, 1)

            def values(h):
                pe.wait_ge(prT_ok, 3 * (h + 1))
                if h % 2 == 0 and h:
                    pe.wait_ge(att_lo, h // 2)
                r = slice(DH * (h % 2), DH * (h % 2 + 1))
                for kt in range(TT):
                    w = T - kt * P
                    last = mm(bank[5][r, kt * P:T], vtok[:, kt, h * DH:(h + 1) * DH], prT[h % 2][:, PT_OFF[kt]:PT_OFF[kt] + w],
                              start=kt == 0, stop=kt == TT - 1)
                last.then_inc(pv_done, 1)

            def out_lru(h):
                c, s = C_OL + h // 2, h // 2
                pe.wait_ge(w_lo, c + 1)
                pe.wait_ge(y_lo, LT)
                if h >= 2:
                    pe.wait_ge(part_ok, h - 1)
                for k in range(LT):
                    w = slice(k * 2 * P + (h % 2) * P, k * 2 * P + (h % 2 + 1) * P)
                    last = three(bank[6 + h % 2][:, :], whi[s][:, w], wlo[s][:, w], mixhi[:, k, :], mixlo[:, k, :],
                                 k == 0, k == LT - 1)
                last.then_inc(fill_done, 1)
                if h % 2 == 1:
                    pe.wait_ge(fill_done, h + 1)
                    pe.sem_inc(chunk_done, 1)

            scores(0)
            pe.wait_ge(v_ok, TT)
            for h in range(HEADS):
                if h + 1 < HEADS:
                    scores(h + 1)
                turn_probs(h)
                out_lru(h)
                values(h)

            OA_BANK = [6, 7, 0, 1, 2, 3, 4, 5]
            pe.wait_ge(part_ok, KD)
            for s in range(4):
                pe.wait_ge(w_lo, C_OA + s + 1)
                for k in range(LT):
                    pe.wait_ge(att_lo, k + 1)
                    for half in range(2):
                        w = slice(k * 2 * P + half * P, k * 2 * P + (half + 1) * P)
                        last = three(bank[OA_BANK[2 * s + half]][:, :], whi[s][:, w], wlo[s][:, w],
                                     mixhi[:, LT + k, :], mixlo[:, LT + k, :], k == 0, k == LT - 1)
                last.then_inc(chunk_done, 1)

            def up(it, first):
                for t in range(2):
                    for half in range(2):
                        c, s = it * 4 + (C_UP + 2 * t + half), 2 * t + half
                        if first:
                            pe.wait_ge(res_add, 6)
                        else:
                            pe.wait_ge((g_out, v_out)[half], it * 2 + (t - 1))
                        channels(c, s, bank[s][:, :], uhi, ulo, 0, KD, True, True,
                                 before=(lambda k: pe.wait_ge(u_lo, KD + k + 1)) if first and t + half == 0 else None)
                        if first and t == 0 and half == 0:
                            pe.wait_ge(acc_ok, KD)
                            mm(bank[7][:, :], ones[:, :], acc[:, :], start=True, stop=True).then_inc(sos_done, 1)

            up(0, True)
            with pe.Fori(1, FT // 2) as it:
                up(it, False)

            with pe.Fori(0, 2) as i:
                for m in range(4):
                    pe.wait_ge(res_add, i * 4 + (KD + m - 3))
                    for s in range(3):
                        pe.wait_ge(act_lo, 8 * (s + 1))
                        channels(i * 12 + (C_DN + 3 * m + s), (3 * m + s) % RING, bank[4 + m][:, :], acthi, actlo,
                                 8 * s, 8, s == 0, s == 2)

            pe.wait_ge(p_in, 16)
            for k in range(2):
                for j in range(TT):
                    last = nc.tensor.transpose(bank[k][:, j * P:(j + 1) * P], ptok[:, j, k * P:(k + 1) * P], ident[:, :])
                last.then_inc(p_t, 1)
            for n in range(2):
                for j in range(TT):
                    if 4 * n + j >= 2:
                        pe.wait_ge(ht_ok, 4 * n + j - 1)
                    if n == 1:
                        pe.wait_ge(res_add, 2 * KD)
                    for c in range(4):
                        last = nc.tensor.transpose(bank[2 + j % 2][:, c * P:(c + 1) * P],
                                                   res[:, 4 * n + c, j * P:(j + 1) * P], ident[:, :])
                    last.then_inc(ht_done, 1)
            pe.wait_ge(acc_ok, 2 * KD)
            pe.wait_ge(pT_ok, 2)
            for j in range(TT):
                last = mm(bank[1][:, j:j + 1], acc[:, j * P:(j + 1) * P], ones[:, 0:1], start=True, stop=True)
            last.then_inc(sos_done, 1)
            pe.wait_ge(p_lo, 2)
            tokens(C_PP, C_PP % RING, bank[4:8], pThi, pTlo, 0, True, True)
            pe.wait_ge(ht_ok, 2 * TT)
            pe.wait_ge(ms_ok, 3)
            tokens(C_PP + 1, (C_PP + 1) % RING, bank[0:4], pThi, pTlo, 0, True, True)
            for n in range(2):
                pe.wait_ge(pp_ok, 4 * (n + 1))
                for s in range(4):
                    pe.wait_ge(u_lo, 2 * KD + 2 * s + 2)
                    tokens(C_PG + 4 * n + s, (C_PG + s) % RING, bank[4:8] if n == 0 else bank[0:4], uhi, ulo, 2 * s,
                           s == 0, s == 3, rows=gate_row if s == 3 else None)
                    if s == 3:
                        pe.wait_ge(gate_row, 4 * n + 4)
                        pe.sem_inc(chunk_done, 1)


_INS = ["x", "p", "ln_mix", "w_in", "conv_w", "conv_b", "gate_a_w", "gate_a_b", "gate_x_w", "gate_x_b", "lru_lambda",
        "q_gain", "k_gain", "w_out", "ln_ffn", "w_up", "ffn_conv_w", "ffn_conv_b", "w_down", "ln_ple", "w_ple_gate",
        "w_ple_proj"]


def kernel(**inputs):
    import numpy as np
    import concourse.bacc as bacc
    from concourse.bass_utils import run_bass_kernel_spmd

    nc = bacc.Bacc("TRN2", target_bir_lowering=False, num_devices=1)
    arrays, args = {}, []
    for name in _INS:
        a = np.ascontiguousarray(inputs[name])
        a = a.reshape(a.shape[2:] if name == "p" else a.shape[1:])
        arrays[f"in_{name}"] = a
        args.append(nc.dram_tensor(f"in_{name}", list(a.shape), mybir.dt.from_np(a.dtype), kind="ExternalInput").ap())
    out = nc.dram_tensor("out", [T, D], F32, kind="ExternalOutput").ap()
    build(nc, *args, out)
    r = run_bass_kernel_spmd(nc, [arrays], core_ids=[0])
    return r.results[0]["out"].reshape(1, T, D)
```

```python
from contextlib import ExitStack

import concourse.bass as bass
from concourse import mybir

F32 = mybir.dt.float32
F32R = mybir.dt.float32r
I32 = mybir.dt.int32
ALU = mybir.AluOpType
ACT = mybir.ActivationFunctionType
AX = mybir.AxisListType

P = 128
T = 512
TT = T // P
D = 1024
KD = D // P
LRU = 512
LT = LRU // P
HEADS = 8
DH = 64
PAIRS = HEADS // 2
FF = 3072
FT = FF // P
PLE = 256
EPS = 1e-6
NEG = -1e30
RING = 4
CW = 1024
KB = 1024

C_XL = 0
C_GL = C_XL + LT
C_Q = C_GL + LT
C_K = C_Q + 4
C_V = C_K + 4
C_OL = C_V + 4
C_OA = C_OL + 4
C_UP = C_OA + 4
C_DN = C_UP + 2 * FT
C_PP = C_DN + 3 * KD
C_PG = C_PP + 2
N_CHUNKS = C_PG + 8

V_LN_MIX, V_CONV_W, V_CONV_B, V_BA, V_BX, V_LAM = 0, 8, 24, 28, 32, 36
V_LN_FFN, V_LN_PLE, V_QG, V_KG, NA = 40, 48, 56, 57, 58
V_FCW, V_FCB, NB = 58, 58 + 3 * FT, 4 * FT
NV = NA + NB

SCORES = [(3, 4, 0), (2, 5, 0), (0, 5, 384), (1, 6, 0)]
TURNED = [(0, 0, 512, (0,)), (512, 1, 512, (1, 3)), (1024, 2, 256, (2,))]
PV_BANK = 7
FILL_BANK = [3, 7, 3, 3, 3, 3, 3, 3]
OA_BANK = [3, 4, 5, 6, 0, 1, 2, 7]
S_OFF = {3: 0, 2: 512, 0: 896, 1: 1024}
PT_OFF = {0: 0, 1: 512, 3: 896, 2: 1024}
S_COLS = 1280


def slope(h):
    return 2.0 ** (-8.0 * (h + 1) / HEADS)


def build(nc, x, p, ln_mix, w_in, conv_w, conv_b, gate_a_w, gate_a_b, gate_x_w, gate_x_b, lru_lambda,
          q_gain, k_gain, w_out, ln_ffn, w_up, ffn_conv_w, ffn_conv_b, w_down, ln_ple, w_ple_gate,
          w_ple_proj, out):
    with ExitStack() as ctx:
        arena = 203 * KB
        base = [nc.sbuf_base + 31 & ~31]

        def at(name, shape, offset, dt=F32):
            return nc.alloc_sbuf_tensor_at(name, shape, dt, offset=base[0] + offset)

        def sem(name):
            return ctx.enter_context(nc.semaphore(name))

        raw = [at(f"raw{s}", [P, CW], 4 * KB * s) for s in range(RING)]
        whi = [at(f"whi{s}", [P, CW], 4 * KB * (4 + s), F32R) for s in range(RING)]
        wlo = [at(f"wlo{s}", [P, CW], 4 * KB * (8 + s), F32R) for s in range(RING)]
        res = at("res", [P, KD, T], 48 * KB)
        uhi = at("uhi", [P, KD, T], 64 * KB, F32R)
        ulo = at("ulo", [P, KD, T], 80 * KB, F32R)
        BIG = 96 * KB
        xtok = at("xtok", [P, TT, D], BIG)
        lx = at("lx", [P, LT, T], BIG)
        lt = at("lt", [P, LT, T], BIG + 8 * KB)
        mixhi = at("mixhi", [P, KD, T], BIG + 16 * KB, F32R)
        mixlo = at("mixlo", [P, KD, T], BIG + 32 * KB, F32R)
        li = at("li", [P, LT, T], BIG + 24 * KB)
        lq = at("lq", [P, LT, T], BIG + 40 * KB)
        qk_tok = [at("qtok", [P, TT, T], BIG + 48 * KB), at("ktok", [P, TT, T], BIG + 56 * KB)]
        prob = [at(f"prob{i}", [P, S_COLS], BIG + (48 + 5 * i) * KB) for i in range(2)]
        prThi = at("prThi", [P, S_COLS], BIG + 58 * KB, F32R)
        prTlo = at("prTlo", [P, S_COLS], BIG + 63 * KB, F32R)
        vs = at("vs", [P, TT, PAIRS, 4 * DH], BIG, F32R)
        vtok = at("vtok", [P, TT, T], BIG + 68 * KB)
        lg = at("lg", [P, LT, T], BIG + 68 * KB)
        qkT = [at("qT", [P, PAIRS, T], BIG + 76 * KB), at("kT", [P, PAIRS, T], BIG + 84 * KB)]
        gw = at("gw", [P, 2, LT, P], BIG + 92 * KB)
        acthi = at("acthi", [P, FT, T], BIG, F32R)
        actlo = at("actlo", [P, FT, T], BIG + 48 * KB, F32R)
        htok = at("htok", [P, TT, D], BIG)
        pp = at("pp", [P, TT, D], BIG + 16 * KB)
        sg = at("sg", [P, TT, D], BIG + 32 * KB)
        fin = at("fin", [P, TT, D], BIG + 48 * KB)
        TMP = 192 * KB
        tmp = at("tmp", [P, 4, T], TMP)
        iota = at("iota", [P, T], TMP, I32)
        rbc = at("rbc", [P, T], 200 * KB)
        dist = at("dist", [P, T], 202 * KB)
        acc = at("acc", [P, T], 202 * KB)
        C0 = 204 * KB
        ident = at("ident", [P, P], C0)
        ones = at("ones", [P, P], C0 + 512)
        vec = at("vec", [P, NV], C0 + 1024)
        sp4 = at("sp4", [P, LT], C0 + 1664)
        small = at("small", [P, 48], C0 + 1696)
        ssq = at("ssq", [P, 2, TT * HEADS], C0 + 1888)
        sm = at("sm", [P, 2, 16], C0 + 2144)
        qg4 = at("qg4", [P, PAIRS], C0 + 2272)
        stage_m = at("stage_m", [KD, P], TMP)
        stage_a = at("stage_a", [NA - KD, P], TMP + 512)
        stage_b = at("stage_b", [NB, P], TMP + 1024)
        junk = [at("junk0", [P, D], TMP + 2 * KB), at("junk1", [P, D], 207 * KB)]
        ptok = at("ptok", [P, TT, PLE], 207 * KB)
        pThi = at("pThi", [P, 2, T], 211 * KB, F32R)
        pTlo = at("pTlo", [P, 2, T], 215 * KB, F32R)
        ss1, rstd1, ss3, rstd3 = (small[:, 4 * i:4 * i + 4] for i in range(4))
        z4, az4, e4, w4, s4, q4, h4 = (small[:, 16 + 4 * i:20 + 4 * i] for i in range(7))
        assert C0 + 2272 + 16 <= 207 * KB and base[0] + 219 * KB <= nc.sbuf_usable_end

        bank = [ctx.enter_context(nc.psum_tensor(f"bank{i}", [P, 512], F32)) for i in range(8)]
        mbank = [bank[i] for i in (3, 4, 0, 1, 2, 5, 6, 7)]

        raw_in = [sem(f"raw_in{s}") for s in range(RING)]
        w_hi, w_lo = sem("w_hi"), sem("w_lo")
        chunk_done = sem("chunk_done")
        x_in = [sem(f"x_in{j}") for j in range(TT)]
        mix_in, stage_in, gw_in, p_in = sem("mix_in"), sem("stage_in"), sem("gw_in"), sem("p_in")
        ident_ok, gw_zero, dist_ok, pool_step = sem("ident_ok"), sem("gw_zero"), sem("dist_ok"), sem("pool_step")
        vec_t, vec_ok, sp_step, sp_ok = sem("vec_t"), sem("vec_ok"), sem("sp_step"), sem("sp_ok")
        exp_lam = sem("exp_lam")
        xt_done, res_ok, u_hi, u_lo = sem("xt_done"), sem("res_ok"), sem("u_hi"), sem("u_lo")
        ss_step, ms_ok, std_ok, rstd_ok = sem("ss_step"), sem("ms_ok"), sem("std_ok"), sem("rstd_ok")
        diag_ok, bc_done, rbc_ok = sem("diag_ok"), sem("bc_done"), sem("rbc_ok")
        xs_ok, tap_ok, conv_step, gs_ok, gelu_ok = (sem(n) for n in ("xs_ok", "tap_ok", "conv_step", "gs_ok", "gelu_ok"))
        gates_done, r_ok, i_ok, tanh_ok, sqrt_ok = (sem(n) for n in ("gates_done", "r_ok", "i_ok", "tanh_ok", "sqrt_ok"))
        den_ok, lru_step, y_ok, y_hi, y_lo = (sem(n) for n in ("den_ok", "lru_step", "y_ok", "y_hi", "y_lo"))
        tok_ok, sq_ok, red_ok, qk_step, qk_ms, qk_std, qk_norm_ok = (
            sem(n) for n in ("tok_ok", "sq_ok", "red_ok", "qk_step", "qk_ms", "qk_std", "qk_norm_ok"))
        qk_t, qkT_ok = sem("qk_t"), sem("qkT_ok")
        vtok_ok, v_hi, v_lo, qg_ok = sem("vtok_ok"), sem("v_hi"), sem("v_lo"), sem("qg_ok")
        s_done, logit_ok, nmax_ok, exp_ok, rinv_ok, prob_ok = (
            sem(n) for n in ("s_done", "logit_ok", "nmax_ok", "exp_ok", "rinv_ok", "prob_ok"))
        pt_done, prT_hi, prT_lo, pv_done = (sem(n) for n in ("pt_done", "prT_hi", "prT_lo", "pv_done"))
        pv_moved, att_ok, att_hi, att_lo = (sem(n) for n in ("pv_moved", "att_ok", "att_hi", "att_lo"))
        half_done = sem("half_done")
        part_ok = sem("part_ok")
        res_add = sem("res_add")
        sqr, acc_ok, sos_done = sem("sqr"), sem("acc_ok"), sem("sos_done")
        g_out, f_tap, f_conv, f_gelu, v_out, f_prod, act_hi, act_lo = (
            sem(n) for n in ("g_out", "f_tap", "f_conv", "f_gelu", "v_out", "f_prod", "act_hi", "act_lo"))
        p_t, p_hi, p_lo, ht_done, ht_ok, pp_ok = (sem(n) for n in ("p_t", "p_hi", "p_lo", "ht_done", "ht_ok", "pp_ok"))
        gate_row, sig_ok, mul_ok, fin_ok, out_done = (sem(n) for n in ("gate_row", "sig_ok", "mul_ok", "fin_ok", "out_done"))

        block = ctx.enter_context(nc.Block())

        @block.sync
        def _(sp):
            def load(c, s, src, shape, first=False):
                if not first:
                    sp.wait_ge(w_lo, c - (RING - 1))
                dst = raw[s][:, :].rearrange("p (k n) -> p k n", k=shape)
                sp.dma_start(dst, src).then_inc(raw_in[s], 16)

            def tile_of(w, r0, nk, c0, nc_):
                return w[r0:r0 + nk * P, bass.ds(c0, nc_)].rearrange("(k p) n -> p k n", p=P)

            def load_x(j):
                sp.dma_start(xtok[:, j, :], x[j * P:(j + 1) * P, :]).then_inc(x_in[j], 16)

            def rows(dst, r, src, n):
                sp.dma_start(dst[r:r + n, :], src.rearrange("(m c) -> m c", c=P)).then_inc(stage_in, 16)

            def load_vectors():
                sp.dma_start(stage_a[V_CONV_W - KD:V_CONV_W - KD + 16, :], conv_w.rearrange("k (m c) -> (k m) c", c=P)).then_inc(stage_in, 16)
                rows(stage_a, V_CONV_B - KD, conv_b, LT)
                rows(stage_a, V_BA - KD, gate_a_b, LT)
                rows(stage_a, V_BX - KD, gate_x_b, LT)
                rows(stage_a, V_LAM - KD, lru_lambda, LT)
                rows(stage_a, V_LN_FFN - KD, ln_ffn, KD)
                rows(stage_a, V_LN_PLE - KD, ln_ple, KD)
                for half in range(2):
                    cols = slice(half * DH, (half + 1) * DH)
                    sp.dma_start(stage_a[V_QG - KD:V_QG - KD + 1, cols], q_gain.rearrange("(o d) -> o d", o=1)).then_inc(stage_in, 16)
                    sp.dma_start(stage_a[V_KG - KD:V_KG - KD + 1, cols], k_gain.rearrange("(o d) -> o d", o=1)).then_inc(stage_in, 16)
                sp.dma_start(stage_b[0:3 * FT, :], ffn_conv_w.rearrange("k (m c) -> (k m) c", c=P)).then_inc(stage_in, 16)
                rows(stage_b, 3 * FT, ffn_conv_b, FT)
                sp.wait_ge(gw_zero, 1)
                for g, w in enumerate((gate_a_w, gate_x_w)):
                    blocks = w.rearrange("(m two) c d -> two c m d", two=2)
                    for half in range(2):
                        sp.dma_start(gw[half * DH:(half + 1) * DH, g, :, half * DH:(half + 1) * DH], blocks[half]).then_inc(gw_in, 16)

            for j in range(TT - 1):
                load_x(j)
            for m in range(2 * LT):
                load(C_XL + m, m % RING, tile_of(w_in, 0, KD, m * P, P), KD, first=m < RING)
                if m == 0:
                    load_x(TT - 1)
                if m == RING - 1:
                    load_vectors()
                    sp.wait_ge(ss_step, TT)
                    sp.dma_start(ptok[:, :, :], p.rearrange("(j p) n -> p j n", p=P)).then_inc(p_in, 16)
            with sp.Fori(0, 3) as t:
                for s in range(4):
                    load(C_Q + s + t * 4, s, tile_of(w_in, 2 * s * P, 2, t * T + 2 * LRU, T), 2)
            for part in range(2):
                for s in range(4):
                    load(C_OL + 4 * part + s, s, tile_of(w_out, part * LRU, LT, s * 2 * P, 2 * P), LT)
            with sp.Fori(0, FT // 2) as i:
                for t in range(2):
                    for half in range(2):
                        load(C_UP + 2 * t + half + i * 4, 2 * t + half,
                             tile_of(w_up, 0, KD, i * (2 * P) + (half * FF + t * P), P), KD)
            with sp.Fori(0, 2) as i:
                for m in range(4):
                    for s in range(3):
                        load(C_DN + 3 * m + s + i * 12, (3 * m + s) % RING,
                             tile_of(w_down, s * D, KD, i * (4 * P) + m * P, P), KD)
            for n in range(2):
                load(C_PP + n, n, tile_of(w_ple_proj, 0, 2, n * T, T), 2)
            for n in range(2):
                for s in range(4):
                    load(C_PG + 4 * n + s, (C_PG + s) % RING, tile_of(w_ple_gate, 2 * s * P, 2, n * T, T), 2)
            for n in range(2):
                for j in range(TT):
                    sp.wait_ge(fin_ok, 4 * n + j + 1)
                    sp.dma_start(out[j * P:(j + 1) * P, n * T:(n + 1) * T], fin[:, j, n * T:(n + 1) * T]).then_inc(out_done, 16)
            sp.wait_ge(out_done, 16 * 2 * TT)

        @block.gpsimd
        def _(pool):
            nc.gpsimd.memset(ident[:, :], 0.0).then_inc(pool_step, 1)
            pool.wait_ge(pool_step, 1)
            nc.gpsimd.affine_select(out=ident[:, :], in_=ident[:, :], compare_op=ALU.not_equal, fill=1.0, base=0,
                                    pattern=[[-1, P]], channel_multiplier=1).then_inc(ident_ok, 1)
            nc.gpsimd.memset(gw[:, :, :, :], 0.0).then_inc(gw_zero, 1)
            nc.gpsimd.memset(ones[:, :], 1.0).then_inc(ident_ok, 1)

            def lo_part(c, s):
                pool.wait_ge(w_hi, c + 1)
                nc.gpsimd.tensor_tensor(wlo[s][:, :], raw[s][:, :], whi[s][:, :].bitcast(F32), ALU.subtract).then_inc(w_lo, 1)

            for c in range(RING):
                if c == 1:
                    pool.wait_ge(raw_in[1], 16)
                    pool.wait_ge(w_hi, 1)
                    nc.gpsimd.tensor_copy(whi[1][:, :], raw[1][:, :]).then_inc(w_hi, 1)
                lo_part(c, c)
            pool.wait_ge(vec_ok, 3)
            pool.wait_ge(ss_step, TT)
            nc.gpsimd.iota(iota[:, :], pattern=[[1, T]], base=-(T - P), channel_multiplier=-1).then_inc(pool_step, 1)
            pool.wait_ge(pool_step, 2)
            nc.gpsimd.tensor_copy(dist[:, :], iota[:, :]).then_inc(pool_step, 1)
            pool.wait_ge(pool_step, 3)
            nc.gpsimd.affine_select(out=dist[:, :], in_=dist[:, :], compare_op=ALU.is_ge, fill=NEG, base=T - P,
                                    pattern=[[-1, T]], channel_multiplier=1).then_inc(dist_ok, 1)
            with pool.Fori(1, N_CHUNKS // RING) as i:
                for s in range(RING):
                    lo_part(s + i * RING, s)
            for c in range(N_CHUNKS // RING * RING, N_CHUNKS):
                lo_part(c, c % RING)

        @block.scalar
        def _(act):
            act.dma_start(stage_m[:, :], ln_mix.rearrange("(m c) -> m c", c=P)).then_inc(mix_in, 16)

            def hi_part(c, s, use_done=True):
                act.wait_ge(raw_in[s], 16 + (c - s) * (16 // RING) if not isinstance(c, int) else 16 * (c // RING + 1))
                if use_done:
                    act.wait_ge(chunk_done, c - (RING - 1))
                nc.scalar.activation(whi[s][:, :], raw[s][:, :], ACT.Copy).then_inc(w_hi, 1)

            for j in range(TT - 1):
                act.wait_ge(x_in[j], 16)
                if j:
                    act.wait_ge(ss_step, j)
                nc.scalar.activation(junk[0][:, :], xtok[:, j, :], ACT.Square, accum_out=ss1[:, j:j + 1]).then_inc(ss_step, 1)
            hi_part(0, 0, use_done=False)

            def keep_x(c):
                act.wait_ge(u_lo, c + 1)
                nc.scalar.activation(res[:, c, :], bank[c][:, :], ACT.Copy).then_inc(res_ok, 1)

            act.wait_ge(vec_ok, 1)
            for c in range(KD):
                act.wait_ge(xt_done, c + 1)
                nc.scalar.activation(uhi[:, c, :], bank[c][:, :], ACT.Copy, scale=vec[:, V_LN_MIX + c:V_LN_MIX + c + 1]).then_inc(u_hi, 1)
                if c == 1:
                    keep_x(0)
            for c in range(1, KD):
                keep_x(c)
            act.wait_ge(w_hi, 2)
            hi_part(2, 2, use_done=False)
            act.wait_ge(ms_ok, 1)
            nc.scalar.activation(rstd1, ss1, ACT.Sqrt).then_inc(std_ok, 1)
            hi_part(3, 3, use_done=False)
            act.wait_ge(sp_step, 1)
            nc.scalar.activation(e4, az4, ACT.Exp, scale=-1.0).then_inc(exp_lam, 1)

            for m in range(LT):
                act.wait_ge(xs_ok, m + 1)
                nc.scalar.activation(lx[:, m, :], lq[:, m, :], ACT.Identity,
                                     bias=vec[:, V_CONV_B + m:V_CONV_B + m + 1],
                                     scale=vec[:, V_CONV_W + 3 * LT + m:V_CONV_W + 3 * LT + m + 1]).then_inc(tap_ok, 1)
                hi_part(4 + m, m)
            for m in range(LT):
                hi_part(8 + m, m)
            for m in range(LT):
                act.wait_ge(gs_ok, m + 1)
                nc.scalar.activation(lg[:, m, :], lg[:, m, :], ACT.Gelu_apprx_tanh).then_inc(gelu_ok, 1)
            act.wait_ge(sp_ok, 1)
            for m in range(LT):
                act.wait_ge(gates_done, m + 1)
                b = 4 + 2 * (m % 2)
                nc.scalar.activation(lt[:, m, :], bank[b][:, :], ACT.Sigmoid, bias=vec[:, V_BA + m:V_BA + m + 1]).then_inc(r_ok, 1)
                nc.scalar.activation(li[:, m, :], bank[b + 1][:, :], ACT.Sigmoid, bias=vec[:, V_BX + m:V_BX + m + 1]).then_inc(i_ok, 1)
                act.wait_ge(r_ok, m + 1)
                nc.scalar.activation(lt[:, m, :], lt[:, m, :], ACT.Tanh, scale=sp4[:, m:m + 1]).then_inc(tanh_ok, 1)
                hi_part(12 + m, m)

            def qk_squares(w):
                for j in range(TT):
                    act.wait_ge(tok_ok, TT * w + j + 1)
                    if w:
                        act.wait_ge(red_ok, j + 1)
                    nc.scalar.activation(tmp[:, j, :], qk_tok[w][:, j, :], ACT.Square).then_inc(sq_ok, 1)

            def qk_sqrt(w):
                act.wait_ge(qk_ms, w + 1)
                nc.scalar.activation(ssq[:, w, :], ssq[:, w, :], ACT.Sqrt).then_inc(qk_std, 1)

            def qk_turned(w):
                if w == 0:
                    act.wait_ge(qg_ok, HEADS)
                for r in range(PAIRS):
                    act.wait_ge(qk_t, PAIRS * w + r + 1)
                    gain = qg4[:, r:r + 1] if w == 0 else vec[:, V_KG:V_KG + 1]
                    nc.scalar.activation(qkT[w][:, r, :], bank[4 * w + r][:, :], ACT.Copy, scale=gain).then_inc(qkT_ok, 1)

            qk_squares(0)
            for m in range(LT):
                act.wait_ge(den_ok, m + 1)
                nc.scalar.activation(lt[:, m, :], lt[:, m, :], ACT.Sqrt).then_inc(sqrt_ok, 1)
            qk_sqrt(0)
            hi_part(16, 0)
            hi_part(17, 1)
            qk_turned(0)
            hi_part(18, 2)
            hi_part(19, 3)
            qk_squares(1)
            qk_sqrt(1)
            for m in range(LT):
                act.wait_ge(y_ok, m + 1)
                nc.scalar.activation(mixhi[:, m, :], lq[:, m, :], ACT.Copy).then_inc(y_hi, 1)
            hi_part(20, 0)
            hi_part(21, 1)
            qk_turned(1)
            hi_part(22, 2)
            hi_part(23, 3)

            def exps(h):
                act.wait_ge(nmax_ok, h + 1)
                for i, _, _ in SCORES:
                    v = prob[h % 2][:, S_OFF[i]:S_OFF[i] + (i + 1) * P]
                    nc.scalar.activation(v, v, ACT.Exp, bias=sm[:, h % 2, 4 + i:5 + i],
                                         accum_out=sm[:, h % 2, 8 + i:9 + i]).then_inc(exp_ok, 1)

            act.wait_ge(chunk_done, C_V + 4)
            act.wait_ge(y_lo, LT)
            for n, j in enumerate((3, 0, 1, 2)):
                nc.scalar.activation(vtok[:, j, :], bank[j][:, :], ACT.Copy, scale=rstd1[:, j:j + 1]).then_inc(vtok_ok, 1)

            def v_view(t, j):
                return t[:, j, :, :].rearrange("p r (e d) -> p r e d", d=DH)[:, :, 0:4:3, :]

            exps(0)
            act.wait_ge(vtok_ok, TT)
            for j in range(TT):
                nc.scalar.activation(v_view(vs, j), vtok[:, j, :].rearrange("p (r e d) -> p r e d", e=2, d=DH),
                                     ACT.Copy).then_inc(v_hi, 1)
            for h in range(HEADS):
                for part, (c0, b, w, _) in enumerate(TURNED):
                    act.wait_ge(pt_done, 3 * h + part + 1)
                    if h and part == 0:
                        act.wait_ge(pv_done, h)
                    nc.scalar.activation(prThi[:, c0:c0 + w], bank[b][:, 0:w], ACT.Copy).then_inc(prT_hi, 1)
                if h + 1 < HEADS:
                    exps(h + 1)
                if h in (1, 2, 4, 6):
                    hi_part(C_OA + h // 2, h // 2)
                act.wait_ge(pv_done, h + 1)
                if h:
                    act.wait_ge(att_ok, h)
                to, of = DH * (h % 2), DH * (1 - h % 2)
                nc.scalar.activation(tmp[to:to + DH, 2, :], bank[PV_BANK][of:of + DH, :], ACT.Copy).then_inc(pv_moved, 1)
                if h % 2 == 1:
                    act.wait_ge(att_ok, h + 1)
                    nc.scalar.activation(mixhi[:, LT + h // 2, :], tmp[:, 3, :], ACT.Copy).then_inc(att_hi, 1)

            def norm_split(m, n, gain):
                act.wait_ge(res_add, n + 1)
                nc.scalar.activation(uhi[:, m, :], res[:, m, :], ACT.Copy, scale=vec[:, bass.ds(m + gain, 1)]).then_inc(u_hi, 1)
                if n >= 4:
                    act.wait_ge(acc_ok, n - 3)
                nc.scalar.activation(tmp[:, m % 4, :], res[:, m, :], ACT.Square).then_inc(sqr, 1)

            for m in range(KD):
                norm_split(m, m, V_LN_FFN)
                if m % 2 == 1:
                    hi_part(C_UP + m // 2, m // 2)
            act.wait_ge(ms_ok, 2)
            nc.scalar.activation(rbc[:, :], rbc[:, :], ACT.Sqrt).then_inc(std_ok, 1)

            def mlp(it):
                for t in range(2):
                    f = it * 2 + t
                    c = it * 4 + (C_UP + 2 * t)
                    hi_part(c + RING, 2 * t)
                    act.wait_ge(g_out, f + 1)
                    act.wait_ge(vec_ok, 3)
                    nc.scalar.activation(tmp[:, 2 + t, :], tmp[:, t, :], ACT.Identity, bias=0.0,
                                         scale=vec[:, bass.ds(f + (V_FCW + 2 * FT), 1)]).then_inc(f_tap, 1)
                    hi_part(c + RING + 1, 2 * t + 1)
                    act.wait_ge(f_conv, f * 2 + 2)
                    act.wait_ge(vec_ok, 3)
                    nc.scalar.activation(tmp[:, 2 + t, :], tmp[:, 2 + t, :], ACT.Gelu_apprx_tanh,
                                         bias=vec[:, bass.ds(f + V_FCB, 1)]).then_inc(f_gelu, 1)
                    act.wait_ge(f_prod, f + 1)
                    act.wait_ge(chunk_done, C_UP)
                    nc.scalar.activation(acthi[:, f, :], tmp[:, 2 + t, :], ACT.Copy).then_inc(act_hi, 1)

            with act.Fori(0, FT // 2) as it:
                mlp(it)
            for k in range(2):
                act.wait_ge(p_t, k + 1)
                nc.scalar.activation(pThi[:, k, :], mbank[k][:, :], ACT.Copy).then_inc(p_hi, 1)
            with act.Fori(0, 2) as i:
                for m in range(4):
                    for s in range(3):
                        hi_part(i * 12 + (C_DN + RING + 3 * m + s), (3 * m + s) % RING)
                    act.wait_ge(acc_ok, i * 4 + (KD + m - 1))
                    act.wait_ge(res_add, i * 4 + (KD + m + 1))
                    act.wait_ge(vec_ok, 3)
                    nc.scalar.activation(uhi[:, i * 4 + m, :], res[:, i * 4 + m, :], ACT.Copy,
                                         scale=vec[:, bass.ds(i * 4 + (V_LN_PLE + m), 1)]).then_inc(u_hi, 1)
                    nc.scalar.activation(tmp[:, 2 + m % 2, :], res[:, i * 4 + m, :], ACT.Square).then_inc(sqr, 1)

            def keep_pp(n):
                act.wait_ge(chunk_done, C_PP + n + 1)
                for j in range(TT):
                    nc.scalar.activation(pp[:, j, n * T:(n + 1) * T], mbank[4 * n + j][:, :], ACT.Copy).then_inc(pp_ok, 1)

            def keep_h(g):
                n, j = divmod(g, TT)
                act.wait_ge(ht_done, g + 1)
                nc.scalar.activation(htok[:, j, n * T:(n + 1) * T], mbank[5 + g % 3][:, :], ACT.Copy).then_inc(ht_ok, 1)

            hi_part(C_PG + 2, C_PP % RING)
            keep_pp(0)
            hi_part(C_PG + 3, (C_PP + 1) % RING)
            keep_pp(1)
            hi_part(C_PG + 4, C_PG % RING)
            act.wait_ge(ms_ok, 3)
            nc.scalar.activation(rstd3, ss3, ACT.Sqrt).then_inc(std_ok, 1)
            for g in range(3):
                keep_h(g)
            hi_part(C_PG + 5, (C_PG + 1) % RING)
            for g in range(3, 6):
                keep_h(g)
            hi_part(C_PG + 6, (C_PG + 2) % RING)
            for g in range(6, 8):
                keep_h(g)
            hi_part(C_PG + 7, (C_PG + 3) % RING)
            act.wait_ge(rstd_ok, 2)
            for n in range(2):
                for j in range(TT):
                    if j < TT - 1:
                        act.wait_ge(gate_row, (TT - 1) * n + j + 1)
                    else:
                        act.wait_ge(chunk_done, C_PG + 4 * (n + 1))
                    nc.scalar.activation(sg[:, j, n * T:(n + 1) * T], mbank[4 * n + j][:, :], ACT.Sigmoid,
                                         scale=rstd3[:, j:j + 1]).then_inc(sig_ok, 1)

        @block.vector
        def _(dve):
            V = nc.vector
            dve.wait_ge(vec_t, 1)
            V.tensor_copy(vec[:, 0:KD], bank[7][:, 0:KD]).then_inc(vec_ok, 1)
            dve.wait_ge(vec_ok, 1)

            def split_u(m, n, gain):
                dve.wait_ge(u_hi, n + 1)
                V.scalar_tensor_tensor(ulo[:, m, :], bank[m][:, :] if gain == V_LN_MIX else res[:, m, :],
                                       vec[:, m + gain:m + gain + 1], uhi[:, m, :].bitcast(F32),
                                       ALU.mult, ALU.subtract).then_inc(u_lo, 1)

            for c in range(KD):
                split_u(c, c, V_LN_MIX)
            V.tensor_tensor_reduce(junk[1][:, :], xtok[:, TT - 1, :], xtok[:, TT - 1, :], 1.0, 0.0, ALU.mult, ALU.add,
                                   ss1[:, TT - 1:TT]).then_inc(ss_step, 1)
            dve.wait_ge(ss_step, TT)
            V.tensor_scalar(ss1, ss1, 1.0 / D, EPS, ALU.mult, ALU.add).then_inc(ms_ok, 1)
            dve.wait_ge(std_ok, 1)
            V.reciprocal(rstd1, rstd1).then_inc(rstd_ok, 1)
            dve.wait_ge(rstd_ok, 1)
            for j in range(TT):
                V.tensor_scalar(tmp[:, 3, j * P:(j + 1) * P], ident[:, :], rstd1[:, j:j + 1], None, ALU.mult).then_inc(diag_ok, 1)
            dve.wait_ge(bc_done, 1)
            V.tensor_copy(rbc[:, :], bank[4][:, :]).then_inc(rbc_ok, 1)
            dve.wait_ge(vec_t, 2)
            V.tensor_copy(vec[:, KD:NA], bank[5][:, 0:NA - KD]).then_inc(vec_ok, 1)
            dve.wait_ge(vec_t, 3)
            V.tensor_copy(vec[:, NA:NV], bank[6][:, 0:NB]).then_inc(vec_ok, 1)
            dve.wait_ge(vec_ok, 3)
            lam = vec[:, V_LAM:V_LAM + LT]
            V.scalar_tensor_tensor(az4, lam, -1.0, lam, ALU.mult, ALU.max).then_inc(sp_step, 1)
            for h in range(HEADS):
                r = slice(DH * (h % 2), DH * (h % 2 + 1))
                V.tensor_scalar(qg4[r, h // 2:h // 2 + 1], vec[r, V_QG:V_QG + 1], float(DH) ** -0.5 / slope(h), None,
                                ALU.mult).then_inc(qg_ok, 1)
            dve.wait_ge(rbc_ok, 1)

            def conv(m):
                dve.wait_ge(tap_ok, m + 1)
                for k in range(1, 4):
                    w = V_CONV_W + (3 - k) * LT + m
                    V.scalar_tensor_tensor(lx[:, m, k:T], lq[:, m, 0:T - k], vec[:, w:w + 1], lx[:, m, k:T],
                                           ALU.mult, ALU.add).then_inc(conv_step, 1)
                    dve.wait_ge(conv_step, 3 * m + k)

            for m in range(LT):
                dve.wait_ge(chunk_done, C_XL + m + 1)
                V.tensor_tensor(lq[:, m, :], bank[m][:, :], rbc[:, :], ALU.mult).then_inc(xs_ok, 1)
                conv(m)
            steps = [1]

            def step(ins):
                ins.then_inc(sp_step, 1)
                steps[0] += 1
                dve.wait_ge(sp_step, steps[0])

            dve.wait_ge(exp_lam, 1)
            step(V.tensor_scalar(w4, e4, 2.0, None, ALU.add))
            step(V.reciprocal(w4, w4))
            step(V.tensor_tensor(s4, e4, w4, ALU.mult))
            step(V.tensor_tensor(q4, s4, s4, ALU.mult))
            step(V.tensor_scalar(h4, q4, 1.0 / 17, None, ALU.mult))
            for k in range(15, 1, -2):
                step(V.scalar_tensor_tensor(h4, h4, 1.0 / k, q4, ALU.add, ALU.mult))
            step(V.scalar_tensor_tensor(h4, h4, 1.0, s4, ALU.add, ALU.mult))
            step(V.tensor_scalar(z4, lam, -1.0, 0.0, ALU.mult, ALU.max))
            step(V.scalar_tensor_tensor(z4, h4, 2.0, z4, ALU.mult, ALU.add))
            V.tensor_scalar(sp4[:, :], z4, 4.0, None, ALU.mult).then_inc(sp_ok, 1)

            for m in range(LT):
                dve.wait_ge(chunk_done, C_GL + m + 1)
                V.tensor_tensor(lg[:, m, :], bank[4 + m][:, :], rbc[:, :], ALU.mult).then_inc(gs_ok, 1)

            n_step = [0]

            def lru_next(ins):
                ins.then_inc(lru_step, 1)
                n_step[0] += 1
                dve.wait_ge(lru_step, n_step[0])

            def den(m):
                dve.wait_ge(tanh_ok, m + 1)
                V.tensor_scalar(lq[:, m, :], lt[:, m, :], 1.0, None, ALU.add).then_inc(den_ok, 1)
                dve.wait_ge(den_ok, m + 1)
                lru_next(V.reciprocal(lq[:, m, :], lq[:, m, :]))
                lru_next(V.tensor_tensor(li[:, m, :], li[:, m, :], lx[:, m, :], ALU.mult))
                lru_next(V.tensor_scalar(lx[:, m, :], lq[:, m, :], 2.0, -1.0, ALU.mult, ALU.add))

            def scan(m):
                dve.wait_ge(sqrt_ok, m + 1)
                lru_next(V.scalar_tensor_tensor(lt[:, m, :], lt[:, m, :], 2.0, lq[:, m, :], ALU.mult, ALU.mult))
                lru_next(V.memset(lt[:, m, 0:1], 1.0))
                lru_next(V.tensor_tensor(li[:, m, :], li[:, m, :], lt[:, m, :], ALU.mult))
                lru_next(V.tensor_tensor_scan(lt[:, m, :], lx[:, m, :], li[:, m, :], 0.0, ALU.mult, ALU.add))
                dve.wait_ge(gelu_ok, m + 1)
                V.tensor_tensor(lq[:, m, :], lt[:, m, :], lg[:, m, :], ALU.mult).then_inc(y_ok, 1)

            def y_split(m):
                dve.wait_ge(y_hi, m + 1)
                V.tensor_tensor(mixlo[:, m, :], lq[:, m, :], mixhi[:, m, :].bitcast(F32), ALU.subtract).then_inc(y_lo, 1)

            def tok_out(w):
                dve.wait_ge(chunk_done, C_Q + 4 * (w + 1))
                for j in range(TT):
                    V.tensor_scalar(qk_tok[w][:, j, :], bank[4 * w + j][:, :], rstd1[:, j:j + 1], None,
                                    ALU.mult).then_inc(tok_ok, 1)

            def qk_sums(w):
                for j in range(TT):
                    dve.wait_ge(sq_ok, TT * w + j + 1)
                    V.tensor_reduce(ssq[:, w, j * HEADS:(j + 1) * HEADS], tmp[:, j, :].rearrange("p (h d) -> p h d", d=DH),
                                    AX.X, ALU.add).then_inc(red_ok, 1)
                dve.wait_ge(red_ok, TT * (w + 1))
                V.tensor_scalar(ssq[:, w, :], ssq[:, w, :], 1.0 / DH, EPS, ALU.mult, ALU.add).then_inc(qk_ms, 1)

            def qk_scale(w):
                dve.wait_ge(qk_std, w + 1)
                V.reciprocal(ssq[:, w, :], ssq[:, w, :]).then_inc(qk_step, 1)
                dve.wait_ge(qk_step, w + 1)
                for j in range(TT):
                    v = qk_tok[w][:, j, :].rearrange("p (h d) -> p h d", d=DH)
                    r = ssq[:, w, j * HEADS:(j + 1) * HEADS].unsqueeze(2).to_broadcast([P, HEADS, DH])
                    V.tensor_tensor(v, v, r, ALU.mult).then_inc(qk_norm_ok, 1)

            for m in range(LT):
                den(m)
            tok_out(0)
            qk_sums(0)
            scan(0)
            qk_scale(0)
            scan(1)
            scan(2)
            scan(3)
            tok_out(1)
            qk_sums(1)
            qk_scale(1)
            for m in range(LT):
                y_split(m)

            def logits(h):
                if h == 0:
                    dve.wait_ge(dist_ok, 1)
                    dve.wait_ge(qk_norm_ok, 2 * TT)
                    dve.wait_ge(qk_t, 2 * PAIRS)
                dve.wait_ge(s_done, h + 1)
                if h >= 2:
                    dve.wait_ge(pt_done, 3 * (h - 1))
                for i, b, c0 in SCORES:
                    w = (i + 1) * P
                    V.tensor_tensor_reduce(prob[h % 2][:, S_OFF[i]:S_OFF[i] + w], bank[b][:, c0:c0 + w],
                                           dist[:, (TT - 1 - i) * P:T], slope(h), 3.0 * NEG, ALU.add, ALU.max,
                                           sm[:, h % 2, i:i + 1]).then_inc(logit_ok, 1)
                dve.wait_ge(logit_ok, 4 * (h + 1))
                V.tensor_scalar(sm[:, h % 2, 4:8], sm[:, h % 2, 0:4], -1.0, None, ALU.mult).then_inc(nmax_ok, 1)

            def normalise(h):
                dve.wait_ge(exp_ok, 4 * (h + 1))
                V.reciprocal(sm[:, h % 2, 12:16], sm[:, h % 2, 8:12]).then_inc(rinv_ok, 1)
                dve.wait_ge(rinv_ok, h + 1)
                for i, _, _ in SCORES:
                    v = prob[h % 2][:, S_OFF[i]:S_OFF[i] + (i + 1) * P]
                    V.tensor_scalar(v, v, sm[:, h % 2, 12 + i:13 + i], None, ALU.mult).then_inc(prob_ok, 1)

            def add_lru(m):
                if m % 2:
                    dve.wait_ge(chunk_done, C_OL + m // 2 + 1)
                else:
                    dve.wait_ge(half_done, m // 2 + 1)
                V.tensor_tensor(res[:, m, :], res[:, m, :], bank[FILL_BANK[m]][:, :], ALU.add).then_inc(part_ok, 1)

            logits(0)
            add_lru(0)
            normalise(0)
            logits(1)
            add_lru(1)

            def split_v(j):
                dve.wait_ge(v_hi, j + 1)
                V.tensor_tensor(vs[:, j, :, DH:3 * DH].rearrange("p r (e d) -> p r e d", d=DH),
                                vtok[:, j, :].rearrange("p (r e d) -> p r e d", e=2, d=DH),
                                vs[:, j, :, :].rearrange("p r (e d) -> p r e d", d=DH)[:, :, 0:4:3, :].bitcast(F32),
                                ALU.subtract).then_inc(v_lo, 1)

            def att_split(pair):
                dve.wait_ge(att_ok, 2 * pair + 2)
                dve.wait_ge(att_hi, pair + 1)
                V.tensor_tensor(mixlo[:, LT + pair, :], tmp[:, 3, :], mixhi[:, LT + pair, :].bitcast(F32),
                                ALU.subtract).then_inc(att_lo, 1)

            dve.wait_ge(vtok_ok, TT)
            split_v(0)
            split_v(1)
            for h in range(HEADS):
                for part, (c0, b, w, _) in enumerate(TURNED):
                    dve.wait_ge(prT_hi, 3 * h + part + 1)
                    V.tensor_tensor(prTlo[:, c0:c0 + w], bank[b][:, 0:w], prThi[:, c0:c0 + w].bitcast(F32),
                                    ALU.subtract).then_inc(prT_lo, 1)
                if h == 0:
                    split_v(2)
                    split_v(3)
                if h in (2, 4):
                    att_split(h // 2 - 1)
                if h + 1 < HEADS:
                    normalise(h + 1)
                if h + 2 < HEADS:
                    add_lru(h + 2)
                dve.wait_ge(pv_moved, h + 1)
                if h % 2 == 0 and h:
                    dve.wait_ge(att_lo, h // 2)
                r = slice(DH * (h % 2), DH * (h % 2 + 1))
                V.tensor_tensor(tmp[r, 3, :], bank[PV_BANK][r, :], tmp[r, 2, :], ALU.add).then_inc(att_ok, 1)
                if h + 2 < HEADS:
                    logits(h + 2)
                if h in (5, 7):
                    att_split(h // 2)

            def add_square(m):
                dve.wait_ge(sqr, m + 1)
                if m == 0:
                    V.tensor_copy(acc[:, :], tmp[:, 0, :]).then_inc(acc_ok, 1)
                else:
                    dve.wait_ge(acc_ok, m)
                    V.tensor_tensor(acc[:, :], acc[:, :], tmp[:, m % 4, :], ALU.add).then_inc(acc_ok, 1)

            dve.wait_ge(part_ok, KD)
            for s in range(4):
                dve.wait_ge(chunk_done, C_OA + s + 1)
                for m in (2 * s, 2 * s + 1):
                    V.tensor_tensor(res[:, m, :], res[:, m, :], bank[OA_BANK[m]][:, :], ALU.add).then_inc(res_add, 1)
                    dve.wait_ge(res_add, m + 1)
                for m in (2 * s, 2 * s + 1):
                    split_u(m, m + KD, V_LN_FFN)
                if s:
                    add_square(2 * s - 2)
                    add_square(2 * s - 1)
            add_square(KD - 2)
            add_square(KD - 1)
            dve.wait_ge(sos_done, 1)
            V.tensor_scalar(rbc[:, :], mbank[4][:, :], 1.0 / D, EPS, ALU.mult, ALU.add).then_inc(ms_ok, 1)
            dve.wait_ge(std_ok, 2)
            V.reciprocal(rbc[:, :], rbc[:, :]).then_inc(rbc_ok, 1)
            dve.wait_ge(rbc_ok, 2)

            def mlp(it, first):
                for t in range(2):
                    f = it * 2 + t
                    c = it * 4 + (C_UP + 2 * t)
                    g, y = tmp[:, t, :], tmp[:, 2 + t, :]
                    dve.wait_ge(chunk_done, c + 1)
                    if not first:
                        dve.wait_ge(f_prod, f - 1)
                    V.tensor_tensor(g, mbank[2 * t][:, :], rbc[:, :], ALU.mult).then_inc(g_out, 1)
                    dve.wait_ge(f_tap, f + 1)
                    for k in range(1, 3):
                        V.scalar_tensor_tensor(y[:, k:T], g[:, 0:T - k], vec[:, bass.ds(f + (V_FCW + (2 - k) * FT), 1)],
                                               y[:, k:T], ALU.mult, ALU.add).then_inc(f_conv, 1)
                        dve.wait_ge(f_conv, f * 2 + k)
                    dve.wait_ge(chunk_done, c + 2)
                    V.tensor_tensor(g, mbank[2 * t + 1][:, :], rbc[:, :], ALU.mult).then_inc(v_out, 1)
                    dve.wait_ge(v_out, f + 1)
                    dve.wait_ge(f_gelu, f + 1)
                    V.tensor_tensor(y, g, y, ALU.mult).then_inc(f_prod, 1)
                    dve.wait_ge(act_hi, f + 1)
                    V.tensor_tensor(actlo[:, f, :], y, acthi[:, f, :].bitcast(F32), ALU.subtract).then_inc(act_lo, 1)

            mlp(0, True)
            with dve.Fori(1, FT // 2) as it:
                mlp(it, False)

            def down(i, m, first):
                dve.wait_ge(chunk_done, i * 12 + (C_DN + 3 * m + 3))
                V.tensor_tensor(res[:, i * 4 + m, :], res[:, i * 4 + m, :], mbank[4 + m][:, :], ALU.add).then_inc(res_add, 1)
                dve.wait_ge(u_hi, i * 4 + (2 * KD + m + 1))
                V.scalar_tensor_tensor(ulo[:, i * 4 + m, :], res[:, i * 4 + m, :], vec[:, bass.ds(i * 4 + (V_LN_PLE + m), 1)],
                                       uhi[:, i * 4 + m, :].bitcast(F32), ALU.mult, ALU.subtract).then_inc(u_lo, 1)
                dve.wait_ge(sqr, i * 4 + (KD + m + 1))
                dve.wait_ge(acc_ok, i * 4 + (KD + m))
                V.tensor_tensor(acc[:, :], acc[:, :], tmp[:, 2 + m % 2, :], ALU.add).then_inc(acc_ok, 1)

            for k in range(2):
                dve.wait_ge(p_hi, k + 1)
                V.tensor_tensor(pTlo[:, k, :], mbank[k][:, :], pThi[:, k, :].bitcast(F32), ALU.subtract).then_inc(p_lo, 1)
            dve.wait_ge(acc_ok, KD)
            V.memset(acc[:, :], 0.0).then_inc(lru_step, 1)
            dve.wait_ge(lru_step, n_step[0] + 1)
            with dve.Fori(0, 2) as i:
                for m in range(4):
                    down(i, m, False)

            dve.wait_ge(sos_done, 2)
            V.tensor_scalar(ss3, mbank[4][:, 0:TT], 1.0 / D, EPS, ALU.mult, ALU.add).then_inc(ms_ok, 1)
            dve.wait_ge(std_ok, 3)
            V.reciprocal(rstd3, rstd3).then_inc(rstd_ok, 1)
            dve.wait_ge(ht_ok, 2 * TT)
            for n in range(2):
                for j in range(TT):
                    s = slice(n * T, (n + 1) * T)
                    k = 4 * n + j + 1
                    dve.wait_ge(sig_ok, k)
                    dve.wait_ge(pp_ok, k)
                    V.tensor_tensor(sg[:, j, s], sg[:, j, s], pp[:, j, s], ALU.mult).then_inc(mul_ok, 1)
                    dve.wait_ge(mul_ok, k)
                    V.tensor_tensor(fin[:, j, s], sg[:, j, s], htok[:, j, s], ALU.add).then_inc(fin_ok, 1)

        @block.tensor
        def _(pe):
            mm = nc.tensor.matmul

            def three(o, ahi, alo, bhi, blo, start, stop):
                mm(o, ahi, bhi, start=start, stop=False)
                mm(o, ahi, blo, start=False, stop=False)
                return mm(o, alo, bhi, start=False, stop=stop)

            def channels(c, s, o, vhi, vlo, k0, n_k, start, stop, w0=0, done=True, before=None):
                pe.wait_ge(w_lo, c + 1)
                for k in range(n_k):
                    if before:
                        before(k)
                    w = slice((w0 + k) * P, (w0 + k + 1) * P)
                    last = three(o, whi[s][:, w], wlo[s][:, w], vhi[:, k0 + k, :], vlo[:, k0 + k, :],
                                 start and k == 0, stop and k == n_k - 1)
                if done:
                    last.then_inc(chunk_done, 1)

            def tokens(c, s, o, vhi, vlo, k0, start, stop, rows=None):
                pe.wait_ge(w_lo, c + 1)
                for j in range(TT):
                    for k in range(2):
                        t, w = slice(j * P, (j + 1) * P), slice(k * T, (k + 1) * T)
                        last = three(o[j][:, :], vhi[:, k0 + k, t], vlo[:, k0 + k, t], whi[s][:, w], wlo[s][:, w],
                                     start and k == 0, stop and k == 1)
                    if j == TT - 1:
                        last.then_inc(chunk_done, 1)
                    elif rows:
                        last.then_inc(rows, 1)

            pe.wait_ge(ident_ok, 1)
            pe.wait_ge(mix_in, 16)
            nc.tensor.transpose(bank[7][:, 0:KD], stage_m[:, :], ident[0:KD, 0:KD]).then_inc(vec_t, 1)
            for j in range(TT):
                pe.wait_ge(x_in[j], 16)
                for c in range(KD):
                    if j == 0 and c == 7:
                        pe.wait_ge(vec_ok, 1)
                    t = nc.tensor.transpose(bank[c][:, j * P:(j + 1) * P], xtok[:, j, c * P:(c + 1) * P], ident[:, :])
                    if j == TT - 1:
                        t.then_inc(xt_done, 1)

            for m in range(LT):
                pe.wait_ge(res_ok, m + 1)
                channels(C_XL + m, m, bank[m][:, :], uhi, ulo, 0, KD, True, True,
                         before=(lambda k: pe.wait_ge(u_lo, k + 1)) if m == 0 else None)
                if m == 1:
                    pe.wait_ge(ident_ok, 2)
                    pe.wait_ge(diag_ok, TT)
                    pe.wait_ge(res_ok, KD)
                    mm(bank[4][:, :], ones[:, :], tmp[:, 3, :], start=True, stop=True).then_inc(bc_done, 1)
                    pe.wait_ge(stage_in, 16 * 13)
                    nc.tensor.transpose(bank[5][:, 0:NA - KD], stage_a[:, :], ident[0:NA - KD, 0:NA - KD]).then_inc(vec_t, 1)
                    nc.tensor.transpose(bank[6][:, 0:NB], stage_b[:, :], ident[0:NB, 0:NB]).then_inc(vec_t, 1)
            pe.wait_ge(vec_ok, 3)
            for m in range(LT):
                channels(C_GL + m, m, bank[4 + m][:, :], uhi, ulo, 0, KD, True, True)
            pe.wait_ge(gw_in, 64)
            pe.wait_ge(xs_ok, LT)
            for s in range(4):
                pe.wait_ge(conv_step, 3 * (s + 1))
                pe.wait_ge(gs_ok, min(2 * s + 2, LT))
                if s >= 2:
                    pe.wait_ge(i_ok, s - 1)
                for g in range(2):
                    last = mm(bank[4 + 2 * (s % 2) + g][:, :], gw[:, g, s, :], lx[:, s, :], start=True, stop=True)
                last.then_inc(gates_done, 1)
                tokens(C_Q + s, s, bank[0:4], uhi, ulo, 2 * s, s == 0, s == 3)

            def turn(w):
                pe.wait_ge(qk_norm_ok, TT * (w + 1))
                for r in range(PAIRS):
                    for j in range(TT):
                        last = nc.tensor.transpose(bank[4 * w + r][:, j * P:(j + 1) * P],
                                                   qk_tok[w][:, j, r * P:(r + 1) * P], ident[:, :])
                    last.then_inc(qk_t, 1)

            pe.wait_ge(i_ok, LT)
            for s in range(4):
                tokens(C_K + s, s, bank[4:8], uhi, ulo, 2 * s, s == 0, s == 3)
                if s == 2:
                    turn(0)
            pe.wait_ge(qkT_ok, PAIRS)
            for s in range(4):
                tokens(C_V + s, s, bank[0:4], uhi, ulo, 2 * s, s == 0, s == 3)
                if s == 2:
                    turn(1)

            def scores(h):
                pe.wait_ge(qkT_ok, 2 * PAIRS)
                if h:
                    pe.wait_ge(logit_ok, 4 * h)
                r = slice(DH * (h % 2), DH * (h % 2 + 1))
                for i, b, c0 in SCORES:
                    w = (i + 1) * P
                    last = mm(bank[b][:, c0:c0 + w], qkT[0][r, h // 2, i * P:(i + 1) * P], qkT[1][r, h // 2, 0:w],
                              start=True, stop=True)
                last.then_inc(s_done, 1)

            def turn_probs(h):
                pe.wait_ge(prob_ok, 4 * (h + 1))
                if h:
                    pe.wait_ge(prT_lo, 3 * h)
                for c0, b, _, key_tiles in TURNED:
                    for kt in key_tiles:
                        for i in range(kt, TT):
                            src = prob[h % 2][:, S_OFF[i] + kt * P:S_OFF[i] + (kt + 1) * P]
                            at_ = PT_OFF[kt] - c0 + (i - kt) * P
                            last = nc.tensor.transpose(bank[b][:, at_:at_ + P], src, ident[:, :])
                    last.then_inc(pt_done, 1)

            def values(h):
                pe.wait_ge(prT_lo, 3 * (h + 1))
                if h:
                    pe.wait_ge(att_ok, h)
                else:
                    pe.wait_ge(part_ok, 2)
                for kt in range(TT):
                    w = T - kt * P
                    if h == 0:
                        pe.wait_ge(v_lo, kt + 1)
                    v = vs[:, kt, h // 2, 2 * DH * (h % 2):2 * DH * (h % 2 + 1)]
                    for n, src in enumerate((prThi, prTlo)):
                        last = mm(bank[PV_BANK][:, kt * P:T], v, src[:, PT_OFF[kt]:PT_OFF[kt] + w],
                                  start=kt == 0 and n == 0, stop=kt == TT - 1 and n == 1)
                last.then_inc(pv_done, 1)

            def out_lru(h):
                c, s = C_OL + h // 2, h // 2
                pe.wait_ge(w_lo, c + 1)
                pe.wait_ge(y_lo, LT)
                pe.wait_ge(vtok_ok, 1)
                if h >= 2:
                    pe.wait_ge(part_ok, h if h > 2 else 1)
                for k in range(LT):
                    w = slice(k * 2 * P + (h % 2) * P, k * 2 * P + (h % 2 + 1) * P)
                    last = three(bank[FILL_BANK[h]][:, :], whi[s][:, w], wlo[s][:, w], mixhi[:, k, :], mixlo[:, k, :],
                                 k == 0, k == LT - 1)
                last.then_inc((half_done, chunk_done)[h % 2], 1)

            def out_att(s, tiles):
                pe.wait_ge(w_lo, C_OA + s + 1)
                for k, half in sorted(((k, half) for k in tiles for half in range(2)), key=lambda o: (o[0] // 2, o[1])):
                    if k == 0 and (s, half) in ((0, 0), (0, 1), (2, 0), (3, 0)):
                        pe.wait_ge(*{(0, 0): (part_ok, KD), (0, 1): (logit_ok, 4 * HEADS), (2, 0): (prT_lo, 3 * HEADS),
                                     (3, 0): (att_ok, HEADS)}[s, half])
                    pe.wait_ge(att_lo, k + 1)
                    w = slice(k * 2 * P + half * P, k * 2 * P + (half + 1) * P)
                    last = three(bank[OA_BANK[2 * s + half]][:, :], whi[s][:, w], wlo[s][:, w],
                                 mixhi[:, LT + k, :], mixlo[:, LT + k, :], k == 0, k == PAIRS - 1)
                if tiles[-1] == PAIRS - 1:
                    last.then_inc(chunk_done, 1)

            scores(0)
            out_lru(0)
            scores(1)
            out_lru(1)
            pe.wait_ge(vtok_ok, TT)
            for h in range(HEADS):
                turn_probs(h)
                if h + 2 < HEADS:
                    out_lru(h + 2)
                else:
                    out_att(h + 2 - HEADS, (0, 1, 2))
                values(h)
                if h + 2 < HEADS:
                    scores(h + 2)
            out_att(2, (0, 1, 2))
            out_att(0, (3,))
            out_att(1, (3,))
            out_att(2, (3,))
            out_att(3, (0, 1, 2, 3))

            late = KD - 2
            for s in range(2):
                pe.wait_ge(res_add, s + 1)
                channels(C_UP + s, s, mbank[s][:, :], uhi, ulo, 0, late, True, False, done=False,
                         before=(lambda k: pe.wait_ge(u_lo, KD + k + 1)) if s == 0 else None)
            for s in range(2):
                channels(C_UP + s, s, mbank[s][:, :], uhi, ulo, late, 2, False, True, w0=late,
                         before=(lambda k: pe.wait_ge(u_lo, KD + late + k + 1)) if s == 0 else None)

            def channel_sum(k):
                if k == 2:
                    pe.wait_ge(acc_ok, KD)
                    mm(mbank[4][:, :], ones[:, :], acc[:, :], start=True, stop=True).then_inc(sos_done, 1)

            for s in range(2, 4):
                channels(C_UP + s, s, mbank[s][:, :], uhi, ulo, 0, KD, True, True,
                         before=channel_sum if s == 2 else None)

            with pe.Fori(1, FT // 2) as it:
                for t in range(2):
                    for half in range(2):
                        s = 2 * t + half
                        pe.wait_ge((g_out, v_out)[half], it * 2 + (t - 1))
                        channels(it * 4 + (C_UP + s), s, mbank[s][:, :], uhi, ulo, 0, KD, True, True)

            pe.wait_ge(p_in, 16)
            pe.wait_ge(g_out, FT - 1)
            pe.wait_ge(v_out, FT - 1)
            for k in range(2):
                for j in range(TT):
                    last = nc.tensor.transpose(mbank[k][:, j * P:(j + 1) * P], ptok[:, j, k * P:(k + 1) * P], ident[:, :])
                last.then_inc(p_t, 1)
            with pe.Fori(0, 2) as i:
                for m in range(4):
                    pe.wait_ge(res_add, i * 4 + (KD + m - 3))
                    for s in range(3):
                        pe.wait_ge(act_lo, 8 * (s + 1))
                        channels(i * 12 + (C_DN + 3 * m + s), (3 * m + s) % RING, mbank[4 + m][:, :], acthi, actlo,
                                 8 * s, 8, s == 0, s == 2)

            pe.wait_ge(p_lo, 2)
            pe.wait_ge(v_out, FT)
            tokens(C_PP, C_PP % RING, mbank[0:4], pThi, pTlo, 0, True, True)
            pe.wait_ge(res_add, 2 * KD)
            tokens(C_PP + 1, (C_PP + 1) % RING, mbank[4:8], pThi, pTlo, 0, True, True)

            def turn_h(g):
                n, j = divmod(g, TT)
                if g >= 3:
                    pe.wait_ge(ht_ok, g - 2)
                for c in range(4):
                    last = nc.tensor.transpose(mbank[5 + g % 3][:, c * P:(c + 1) * P], res[:, 4 * n + c, j * P:(j + 1) * P],
                                               ident[:, :])
                last.then_inc(ht_done, 1)

            for n in range(2):
                pe.wait_ge(pp_ok, 4)
                if n == 1:
                    pe.wait_ge(ht_ok, 2 * TT)
                    pe.wait_ge(ms_ok, 3)
                for s in range(4):
                    pe.wait_ge(u_lo, 2 * KD + 2 * s + 2)
                    tokens(C_PG + 4 * n + s, (C_PG + s) % RING, mbank[4 * n:4 * n + 4], uhi, ulo, 2 * s,
                           s == 0, s == 3, rows=gate_row if s == 3 else None)
                    if n == 0 and s == 0:
                        pe.wait_ge(acc_ok, 2 * KD)
                        pe.wait_ge(pp_ok, 2 * TT)
                        for j in range(TT):
                            last = mm(mbank[4][:, j:j + 1], acc[:, j * P:(j + 1) * P], ones[:, 0:1], start=True, stop=True)
                        last.then_inc(sos_done, 1)
                    if n == 0 and s < 3:
                        for g in range(3 * s, min(3 * s + 3, 2 * TT)):
                            turn_h(g)


_INS = ["x", "p", "ln_mix", "w_in", "conv_w", "conv_b", "gate_a_w", "gate_a_b", "gate_x_w", "gate_x_b", "lru_lambda",
        "q_gain", "k_gain", "w_out", "ln_ffn", "w_up", "ffn_conv_w", "ffn_conv_b", "w_down", "ln_ple", "w_ple_gate",
        "w_ple_proj"]


def kernel(**inputs):
    import numpy as np
    import concourse.bacc as bacc
    from concourse.bass_utils import run_bass_kernel_spmd

    nc = bacc.Bacc("TRN2", target_bir_lowering=False, num_devices=1, dynamic_dma_scratch_size=1024)
    arrays, args = {}, []
    for name in _INS:
        a = np.ascontiguousarray(inputs[name])
        a = a.reshape(a.shape[2:] if name == "p" else a.shape[1:])
        arrays[f"in_{name}"] = a
        args.append(nc.dram_tensor(f"in_{name}", list(a.shape), mybir.dt.from_np(a.dtype), kind="ExternalInput").ap())
    out = nc.dram_tensor("out", [T, D], F32, kind="ExternalOutput").ap()
    build(nc, *args, out)
    r = run_bass_kernel_spmd(nc, [arrays], core_ids=[0])
    return r.results[0]["out"].reshape(1, T, D)
```
